# Optimizing a Trainium2 kernel written in Bass

```python
import math
import jax, jax.numpy as jnp
from jax import lax
import numpy as np

D_MODEL = 1024
BATCH = 1
SEQ = 256
DEPTH = 1

HEAD_DIM = 64
N_HEADS_MOBA = 8
N_HEADS_RWKV = 8
W_MOBA = N_HEADS_MOBA * HEAD_DIM
W_RWKV = N_HEADS_RWKV * HEAD_DIM
MOBA_BLOCK = 256
MOBA_TOPK = 3
Q_CHUNK = 32
NUM_BUCKETS = 32
MAX_DISTANCE = 1024
D_FF = 2816
DECAY_LORA = 64
AAA_LORA = 64
GATE_LORA = 160
RMS_EPS = 1e-6
GN_EPS = HEAD_DIM * 1e-5
IN_COLS = 3 * W_MOBA + 3 * W_RWKV + 2 * D_MODEL

kernel_name = "hybrid_moba_rwkv7_macaron"

def rms_norm(x, g):
    xf = x.astype(jnp.float32)
    y = xf * lax.rsqrt(jnp.mean(xf * xf, axis=-1, keepdims=True) + RMS_EPS)
    return (y * g.astype(jnp.float32)).astype(x.dtype)

def swiglu(h, w_gate, w_up, w_down):
    return (jax.nn.silu(h @ w_gate) * (h @ w_up)) @ w_down

def t5_bucket(dist):
    n = jnp.maximum(dist, 0)
    max_exact = NUM_BUCKETS // 2
    nf = jnp.maximum(n, max_exact).astype(jnp.float32)
    large = max_exact + (jnp.log(nf / max_exact) / math.log(MAX_DISTANCE / max_exact)
                         * (NUM_BUCKETS - max_exact)).astype(jnp.int32)
    large = jnp.minimum(large, NUM_BUCKETS - 1)
    return jnp.where(n < max_exact, n, large)

def shift_seq(z):
    return jnp.pad(z, ((0, 0), (1, 0), (0, 0)))[:, :-1]

def moba_attention(q, k, v, rel_bias):
    B, S, H, D = q.shape
    nb = -(-S // MOBA_BLOCK)
    s_pad = nb * MOBA_BLOCK
    pad = ((0, 0), (0, 0), (0, s_pad - S), (0, 0))
    q = jnp.pad(q.transpose(0, 2, 1, 3), pad)
    k = jnp.pad(k.transpose(0, 2, 1, 3), pad)
    v = jnp.pad(v.transpose(0, 2, 1, 3), pad)
    k_blocks = k.reshape(B, H, nb, MOBA_BLOCK, D)
    v_blocks = v.reshape(B, H, nb, MOBA_BLOCK, D)
    k_mean = jnp.mean(k_blocks.astype(jnp.float32), axis=3)
    topk = min(MOBA_TOPK, max(nb - 1, 1))
    n_chunks = s_pad // Q_CHUNK
    q_chunks = q.reshape(B, H, n_chunks, Q_CHUNK, D).transpose(2, 0, 1, 3, 4)
    bias_t = rel_bias.T
    head_ids = jnp.arange(H)[None, :, None, None, None]
    scale = D ** -0.5
    gather = jax.vmap(jax.vmap(lambda blocks, ix: blocks[ix]))
    key_off = jnp.arange(MOBA_BLOCK)

    def chunk(args):
        q_c, c = args
        start = c * Q_CHUNK
        t = start + jnp.arange(Q_CHUNK)
        blk = start // MOBA_BLOCK
        gate = jnp.einsum('bhqd,bhnd->bhqn', q_c.astype(jnp.float32), k_mean)
        gate = jnp.where(jnp.arange(nb) < blk, gate, -jnp.inf)
        _, idx = lax.top_k(gate, topk)
        valid = idx < blk
        k_sel = gather(k_blocks, idx)
        v_sel = gather(v_blocks, idx)
        kpos_sel = idx[..., None] * MOBA_BLOCK + key_off
        bias_sel = bias_t[head_ids, t5_bucket(t[:, None, None] - kpos_sel)]
        s_sel = (jnp.einsum('bhqd,bhqmkd->bhqmk', q_c, k_sel).astype(jnp.float32) * scale
                 + bias_sel.astype(jnp.float32))
        s_sel = jnp.where(valid[..., None], s_sel, -jnp.inf)
        k_own = lax.dynamic_index_in_dim(k_blocks, blk, axis=2, keepdims=False)
        v_own = lax.dynamic_index_in_dim(v_blocks, blk, axis=2, keepdims=False)
        dist_own = t[:, None] - (blk * MOBA_BLOCK + key_off)[None, :]
        bias_own = bias_t[:, t5_bucket(dist_own)]
        s_own = (jnp.einsum('bhqd,bhkd->bhqk', q_c, k_own).astype(jnp.float32) * scale
                 + bias_own.astype(jnp.float32))
        s_own = jnp.where(dist_own >= 0, s_own, -jnp.inf)
        logits = jnp.concatenate(
            [s_sel.reshape(B, H, Q_CHUNK, topk * MOBA_BLOCK), s_own], axis=-1)
        p = jax.nn.softmax(logits, axis=-1).astype(v.dtype)
        p_sel = p[..., :topk * MOBA_BLOCK].reshape(B, H, Q_CHUNK, topk, MOBA_BLOCK)
        p_own = p[..., topk * MOBA_BLOCK:]
        return (jnp.einsum('bhqmk,bhqmkd->bhqd', p_sel, v_sel)
                + jnp.einsum('bhqk,bhkd->bhqd', p_own, v_own))

    out = lax.map(chunk, (q_chunks, jnp.arange(n_chunks)))
    out = out.transpose(1, 0, 3, 2, 4).reshape(B, s_pad, H, D)[:, :S]
    return out.reshape(B, S, H * D)

def _rwkv_step(state, inp):
    r_t, w_t, k_t, v_t, a_t, b_t = inp
    sa = jnp.einsum('bhvk,bhk->bhv', state, a_t)
    state = (state * w_t[:, :, None, :] + sa[..., None] * b_t[:, :, None, :]
             + v_t[..., None] * k_t[:, :, None, :])
    y = jnp.einsum('bhvk,bhk->bhv', state, r_t)
    return state, y

def rwkv7_time_mix(h, r_p, k_p, v_p, mix_rkv, mix_wag, w_lora_a, w_lora_b, w0,
                   a_lora_a, a_lora_b, a0, g_lora_a, g_lora_b, k_k, k_a, r_k,
                   ln_x_w, ln_x_b):
    B, S, _ = h.shape
    H, N = N_HEADS_RWKV, HEAD_DIM
    r = r_p + (shift_seq(r_p) - r_p) * mix_rkv[0]
    k = k_p + (shift_seq(k_p) - k_p) * mix_rkv[1]
    v = v_p + (shift_seq(v_p) - v_p) * mix_rkv[2]
    dh = shift_seq(h) - h
    xw = h + dh * mix_wag[0]
    xa = h + dh * mix_wag[1]
    xg = h + dh * mix_wag[2]
    w_raw = -jax.nn.softplus(-(w0 + jnp.tanh(xw @ w_lora_a) @ w_lora_b)) - 0.5
    decay = jnp.exp(-jnp.exp(w_raw.astype(jnp.float32)))
    a = jax.nn.sigmoid(a0 + (xa @ a_lora_a) @ a_lora_b)
    g = jax.nn.sigmoid(xg @ g_lora_a) @ g_lora_b
    kk = (k * k_k).reshape(B, S, H, N).astype(jnp.float32)
    kk = kk / jnp.maximum(jnp.linalg.norm(kk, axis=-1, keepdims=True), 1e-12)
    k = k * (1.0 + (a - 1.0) * k_a)
    heads = lambda z: z.reshape(B, S, H, N).astype(jnp.float32)
    r_h, k_h, v_h, a_h, w_h = heads(r), heads(k), heads(v), heads(a), heads(decay)
    tb = lambda z: z.transpose(1, 0, 2, 3)
    state0 = jnp.zeros((B, H, N, N), jnp.float32)
    _, y = lax.scan(_rwkv_step, state0,
                    (tb(r_h), tb(w_h), tb(k_h), tb(v_h), tb(-kk), tb(kk * a_h)))
    y = y.transpose(1, 0, 2, 3)
    mu = jnp.mean(y, axis=-1, keepdims=True)
    var = jnp.mean(jnp.square(y - mu), axis=-1, keepdims=True)
    y = ((y - mu) * lax.rsqrt(var + GN_EPS)).reshape(B, S, H * N)
    y = y * ln_x_w.astype(jnp.float32) + ln_x_b.astype(jnp.float32)
    bonus = jnp.sum(r_h * k_h * r_k.astype(jnp.float32), axis=-1, keepdims=True) * v_h
    y = (y + bonus.reshape(B, S, H * N)).astype(h.dtype)
    return y * g

def _dense(k, shape, fan_in, scale=1.0):
    return jax.random.normal(k, shape, jnp.float32) * (scale * fan_in ** -0.5)

def setup_inputs(seed: int = 0) -> dict:
    key = jax.random.key(seed)
    ks = iter(jax.random.split(key, 48))
    L, D = DEPTH, D_MODEL
    nrm = lambda shape, s: s * jax.random.normal(next(ks), shape, jnp.float32)
    uni = lambda shape, lo, hi: jax.random.uniform(next(ks), shape, jnp.float32, lo, hi)
    return {
        "x": jax.random.normal(next(ks), (BATCH, SEQ, D), jnp.float32),
        "rel_bias": nrm((NUM_BUCKETS, N_HEADS_MOBA), 0.1),
        "norm_ffn1": 1.0 + nrm((L, D), 0.05),
        "ffn1_gate": _dense(next(ks), (L, D, D_FF), D),
        "ffn1_up": _dense(next(ks), (L, D, D_FF), D),
        "ffn1_down": _dense(next(ks), (L, D_FF, D), D_FF),
        "norm_mix": 1.0 + nrm((L, D), 0.05),
        "w_in": _dense(next(ks), (L, D, IN_COLS), D),
        "mix_rkv": uni((L, 3, W_RWKV), 0.0, 1.0),
        "mix_wag": uni((L, 3, D), 0.0, 1.0),
        "w_lora_a": _dense(next(ks), (L, D, DECAY_LORA), D),
        "w_lora_b": _dense(next(ks), (L, DECAY_LORA, W_RWKV), DECAY_LORA, 0.1),
        "w0": uni((L, W_RWKV), -6.5, -1.5),
        "a_lora_a": _dense(next(ks), (L, D, AAA_LORA), D),
        "a_lora_b": _dense(next(ks), (L, AAA_LORA, W_RWKV), AAA_LORA, 0.1),
        "a0": nrm((L, W_RWKV), 0.1),
        "g_lora_a": _dense(next(ks), (L, D, GATE_LORA), D),
        "g_lora_b": _dense(next(ks), (L, GATE_LORA, W_RWKV), GATE_LORA),
        "k_k": 0.85 + nrm((L, W_RWKV), 0.05),
        "k_a": 1.0 + nrm((L, W_RWKV), 0.05),
        "r_k": nrm((L, N_HEADS_RWKV, HEAD_DIM), 0.1),
        "ln_x_w": 1.0 + nrm((L, W_RWKV), 0.05),
        "ln_x_b": nrm((L, W_RWKV), 0.02),
        "proj_a": _dense(next(ks), (L, W_MOBA, D), W_MOBA),
        "proj_b": _dense(next(ks), (L, W_RWKV, D), W_RWKV),
        "w_out": _dense(next(ks), (L, D, D), D),
        "norm_ffn2": 1.0 + nrm((L, D), 0.05),
        "ffn2_gate": _dense(next(ks), (L, D, D_FF), D),
        "ffn2_up": _dense(next(ks), (L, D, D_FF), D),
        "ffn2_down": _dense(next(ks), (L, D_FF, D), D_FF),
        "norm_final": 1.0 + nrm((D,), 0.05),
    }

def reference(x, rel_bias, norm_ffn1, ffn1_gate, ffn1_up, ffn1_down, norm_mix, w_in,
              mix_rkv, mix_wag, w_lora_a, w_lora_b, w0, a_lora_a, a_lora_b, a0,
              g_lora_a, g_lora_b, k_k, k_a, r_k, ln_x_w, ln_x_b, proj_a, proj_b, w_out,
              norm_ffn2, ffn2_gate, ffn2_up, ffn2_down, norm_final):
    B, S, _ = x.shape
    splits = list(np.cumsum([W_MOBA, W_MOBA, W_MOBA, W_RWKV, W_RWKV, W_RWKV, D_MODEL])[:])
    for l in range(DEPTH):
        x = x + 0.5 * swiglu(rms_norm(x, norm_ffn1[l]), ffn1_gate[l], ffn1_up[l], ffn1_down[l])
        h = rms_norm(x, norm_mix[l])
        proj = h @ w_in[l]
        qa, ka, va, rb, kb, vb, ga, gb = jnp.split(proj, splits, axis=-1)
        to_heads = lambda z: z.reshape(B, S, N_HEADS_MOBA, HEAD_DIM)
        y_a = moba_attention(to_heads(qa), to_heads(ka), to_heads(va), rel_bias)
        y_b = rwkv7_time_mix(h, rb, kb, vb, mix_rkv[l], mix_wag[l], w_lora_a[l], w_lora_b[l],
                             w0[l], a_lora_a[l], a_lora_b[l], a0[l], g_lora_a[l],
                             g_lora_b[l], k_k[l], k_a[l], r_k[l], ln_x_w[l], ln_x_b[l])
        merged = jax.nn.sigmoid(ga) * (y_a @ proj_a[l]) + jax.nn.sigmoid(gb) * (y_b @ proj_b[l])
        x = x + merged @ w_out[l]
        x = x + 0.5 * swiglu(rms_norm(x, norm_ffn2[l]), ffn2_gate[l], ffn2_up[l], ffn2_down[l])
    return rms_norm(x, norm_final)


_drawn_inputs = setup_inputs


def setup_inputs(seed=0):
    import zlib

    import numpy as np

    out = dict(_drawn_inputs(seed))
    spreads = {}
    factors = {'rel_bias': 6.669,
     'w_lora_a': 8.0,
     'w_lora_b': 8.0,
     'a_lora_a': 4.762,
     'a_lora_b': 4.783,
     'a0': 4.563,
     'k_k': 5.559,
     'k_a': 3.994,
     'ln_x_w': 4.118,
     'ln_x_b': 8.0,
     'norm_ffn2': 2.935}
    for name, (base, spread) in spreads.items():
        noise = np.random.default_rng([zlib.crc32(name.encode()), seed]).standard_normal(out[name].shape)
        drawn = base * np.exp(spread * noise) if base else spread * noise
        out[name] = __import__('jax').numpy.asarray(drawn.astype(out[name].dtype))
    for name, factor in factors.items():
        out[name] = (out[name] * factor).astype(out[name].dtype)
    return out
```

```python
from contextlib import ExitStack

import concourse.bass as bass
from concourse import mybir
import numpy as np

F32 = mybir.dt.float32
F32R = mybir.dt.float32r
ALU = mybir.AluOpType
ACT = mybir.ActivationFunctionType

P = 128
T = 256
D = 1024
KD = D // P
FF = 2816
FT = FF // P
W = 256
H = 8
HD = 64
WM = H * HD
HT = WM // P
C = 64
NCH = T // C
DL, AL, GL = 64, 64, 160
NB, MAXD = 32, 1024
RMS_EPS = 1e-6
GN_EPS = HD * 1e-5
NEG = -1e30
KS = (8, 8, 6)
NDOWN = len(KS) * D // W
EXP_HALF = float(np.exp(-0.5))

N_FFN1 = 0
N_DOWN1 = N_FFN1 + 2 * FF // W
N_RKV = N_DOWN1 + NDOWN
N_QK = N_RKV + 3 * WM // W
N_V = N_QK + 2 * WM // W
N_GATE = N_V + WM // W
N_PROJ = N_GATE + 2 * D // W
N_OUT = N_PROJ + D // W
N_FFN2 = N_OUT + D // W
N_DOWN2 = N_FFN2 + 2 * FF // W
N_ALL = N_DOWN2 + NDOWN

VECS = {}
for _name, _cols in (("norm_ffn1", KD), ("norm_mix", KD), ("norm_ffn2", KD), ("norm_final", KD),
                     ("mix_wag", 3 * KD), ("mix_rkv", 3 * HT), ("w0", HT), ("a0", HT), ("k_k", HT),
                     ("k_a", HT), ("r_k", HT), ("ln_x_w", HT), ("ln_x_b", HT)):
    VECS[_name] = (sum(c for _, c in VECS.values()), _cols)
NVEC = sum(c for _, c in VECS.values())

CONSTS = ("ident", "flip", "mean_d", "head_sum", "head_mean", "low_a", "low_r", "g2", "lev2", "lev4",
          "lev8", "lev16", "lev32")
CCOL = {name: i * P for i, name in enumerate(CONSTS)}
C_SUI, C_EPS = len(CONSTS) * P, len(CONSTS) * P + HD
C_HOT = C_EPS + 2
C_NEG = C_HOT + 384
C_ALL = C_NEG + 384


def shape_constants():
    c = np.zeros((P, C_ALL), np.float32)
    i = np.arange(P)[:, None]
    j = np.arange(P)[None, :]
    same = i // C == j // C
    eye = i == j
    mats = {
        "ident": eye, "flip": i + j == P - 1, "mean_d": np.full((P, P), 1.0 / D),
        "head_sum": i // HD == j // HD, "head_mean": (i // HD == j // HD) / HD,
        "low_a": same & (i < j), "low_r": same & (i <= j),
        "g2": eye | ((i // 2 == j // 2) & (i < j)),
    }
    for b in (2, 4, 8, 16, 32):
        mats[f"lev{b}"] = eye | ((i // (2 * b) == j // (2 * b)) & (i // b % 2 == 1) & (j // b % 2 == 0))
    for name, m in mats.items():
        c[:, CCOL[name]:CCOL[name] + P] = m
    c[:, C_SUI:C_SUI + HD] = i % HD == np.arange(HD)[None, :]
    c[:, C_EPS], c[:, C_EPS + 1] = RMS_EPS, GN_EPS
    dist = T - 1 - np.arange(384)
    n = np.maximum(dist, 0)
    exact = NB // 2
    large = exact + (np.log(np.maximum(n, exact).astype(np.float32) / np.float32(exact))
                     / np.float32(np.log(MAXD / exact)) * np.float32(NB - exact)).astype(np.int32)
    bucket = np.where(n < exact, n, np.minimum(large, NB - 1))
    c[:NB, C_HOT:C_HOT + 384] = np.arange(NB)[:, None] == bucket[None, :]
    c[:H, C_NEG:C_NEG + 384] = np.where(dist < 0, NEG, 0.0)[None, :]
    return c


SIGNALS = """
x_in vec_in const_in vecT x_T x_loaded vec_ready
hi_ready lo_ready multiplied
squares mean_sq rms_ready rstd_ready h_ready hhi_ready hlo_ready
silu_done hid_prod hid_hi hid_lo down_first x_ffn_even x_ffn_odd
bias_row bias_row_sb bias_out bias_in bias_flip bias_ready
lora_in pads_zero h_diff xw_ready xa_ready xg_ready
mix_taken
tw_done ta_done tg_done tw_ready ta_ready tg_ready
z_done a_done g_done sig_w a_ready g_ready decay_ready scan_inputs
dve_chain kk_sq_in kk_sq kk_ss kk_norm rkk_ready rkk_sum bonus_done
ab_ready v_ready kc_ready
s_done logits negmax exp_done prob_ready pt_done pt_ready pv_done ya_hi ya_lo
vt_done vt_ready tok_done tok_ready
pair_done pair_ready n_ready g2_ready t2_done
u_done iu_ready level_done t2_ready inv_ready invT_ready
x1_done as_done as_ready rh_done rh_ready phi_done phi_ready st_done st_ready
y_done y_ready gmean gdiff gsq gvar gstd yb_ready yb_hi yb_lo
merged m_hi m_lo x_mix
final_T final_copied final_copied_act out_stored
""".split()


def trunk(nc, A, consts, out):
    bias_dram = nc.dram_tensor("bias_rows", (H, 384), F32, kind="Internal").ap()
    with ExitStack() as ctx:
        def sb(name, shape, dt=F32, scope=ctx):
            return scope.enter_context(nc.sbuf_tensor(name, shape, dt))

        sg = {n: ctx.enter_context(nc.semaphore(n)) for n in SIGNALS}
        w_landed = [ctx.enter_context(nc.semaphore(f"w_landed{i}")) for i in range(2)]
        bank = [ctx.enter_context(nc.psum_tensor(f"bank{i}", [P, 512], F32)) for i in range(8)]

        raw = [sb(f"w_raw{i}", [P, KD, W]) for i in range(2)]
        whi = [sb(f"w_hi{i}", [P, KD, W], F32R) for i in range(2)]
        wlo = [sb(f"w_lo{i}", [P, KD, W], F32R) for i in range(2)]
        x = sb("x", [P, KD, T])
        cst = sb("cst", [P, C_ALL])
        vec = sb("vec", [P, NVEC])
        rms = sb("rms", [P, T])
        rstd = sb("rstd", [P, T])
        bias_sb = sb("bias_sb", [H, 384])
        idle = sb("idle", [P, 2])

        def mat(name):
            return cst[:, CCOL[name]:CCOL[name] + P]

        ident, flip = mat("ident"), mat("flip")

        def v(name, i):
            return vec[:, VECS[name][0] + i:VECS[name][0] + i + 1]

        with ExitStack() as sc:
            x_tok = sb("x_tok", [P, 2, D], scope=sc)
            vec_rows = sb("vec_rows", [NVEC, P], scope=sc)
            rel = sb("rel", [NB, H], scope=sc)

        with ExitStack() as sc:
            h_f = sb("h_f", [P, KD, T], scope=sc)
            hhi_f = sb("hhi_f", [P, KD, T], F32R, scope=sc)
            hlo_f = sb("hlo_f", [P, KD, T], F32R, scope=sc)
            silu = sb("silu", [P, 2, T], scope=sc)
            prod = sb("prod", [P, 2, T], scope=sc)
            hid_hi = sb("hid_hi_t", [P, FT, T], F32R, scope=sc)
            hid_lo = sb("hid_lo_t", [P, FT, T], F32R, scope=sc)
            out_tok = sb("out_tok", [P, 2, D], scope=sc)

        with ExitStack() as mix:
            def mb(name, shape, dt=F32, scope=mix):
                return sb(name, shape, dt, scope)

            r = mb("r", [P, HT, T])
            k = mb("k", [P, HT, T])
            vv = mb("v", [P, HT, T])
            dec = mb("dec", [P, HT * NCH, C + 1])
            one = mb("one", [P, HT * NCH, C + 1])
            run = mb("run", [P, HT * NCH, C + 1])
            kkn = mb("kkn", [P, HT, T])
            tmp = mb("tmp", [P, HT, T])
            aa = mb("aa", [P, HT, T])
            AR = mb("AR", [P, 2, HT, T])
            kt = mb("kt", [P, HT, T])
            gg = mb("gg", [P, HT, T])
            gates = mb("gates", [P, 2 * KD, T])
            yahi = mb("yahi", [P, HT, T], F32R)
            yalo = mb("yalo", [P, HT, T], F32R)
            inv_run = dec[:, :, 0:C]
            dpc = one[:, :, 0:C]
            bc, kc = kkn, tmp
            xa0, xa1 = gates[:, 0:KD], gates[:, KD:2 * KD]
            diff = AR[:, :, :, :].rearrange("p a j t -> p (a j) t")
            run_t = run[:, :, 1:C + 1]
            run_before = run[:, :, 0:C]
            run_end = run[:, :, C:C + 1]
            with ExitStack() as sc:
                h_m = mb("h_m", [P, KD, T + 1], scope=sc)
                hhi_m = mb("hhi_m", [P, KD, T], F32R, scope=sc)
                hlo_m = mb("hlo_m", [P, KD, T], F32R, scope=sc)
                rkv = mb("rkv", [P, 3 * HT, T + 1], scope=sc)
                tws = mb("tws", [DL, T], scope=sc)
                tas = mb("tas", [AL, T], scope=sc)
                tg0 = mb("tg0", [P, T], scope=sc)
                tg1 = mb("tg1", [GL - P, T], scope=sc)
                with ExitStack() as sc2:
                    laB = mb("laB", [AL, 2 * WM], scope=sc2)[:, 0:WM]
                    lgA = mb("lgA", [P, KD, GL], scope=sc2)
                flat = aa[:].rearrange("p j t -> p (j t)")
                lwA = flat[:, 0:KD * DL].rearrange("p (c n) -> p c n", c=KD)
                laA = flat[:, KD * DL:2 * KD * DL].rearrange("p (c n) -> p c n", c=KD)
                lwB = run[:].rearrange("p a b -> p (a b)")[0:DL, 0:WM]
                flat = gg[:].rearrange("p j t -> p (j t)")
                lgB0, lgB1 = flat[:, 0:WM], flat[0:GL - P, WM:2 * WM]
                qk = mb("qk", [P, 2 * HT, T], scope=sc)
                va = mb("va", [P, 2, WM], scope=sc)
            with ExitStack() as sc:
                bias_w = mb("bias_w", [P, H, T], scope=sc)
                bias = mb("bias", [P, H, T], scope=sc)
                lg = mb("lg", [P, 2, 3 * P], scope=sc)
                pt = mb("pt", [P, 2, 3 * P], scope=sc)
                stat = mb("stat", [P, H, 8], scope=sc)
            with ExitStack() as sc:
                vt = mb("vt", [P, 2, WM], scope=sc)
                bct = mb("bct", [P, 2, WM], scope=sc)
                kct = mb("kct", [P, 2, WM], scope=sc)
                NR = mb("NR", [P, H, 2, P], scope=sc)
                KK = mb("KK", [P, H, 2, P], scope=sc)
                G = mb("G", [P, H, P], scope=sc)
                TT = mb("TT", [P, H, P], scope=sc)
                IU = mb("IU", [P, H, P], scope=sc)
                phi = mb("phi", [P, 2, 2, HT, C], scope=sc)
                state = mb("state", [P, NCH, HT, C], scope=sc)
                AX = mb("AX", [P, 2, H, P], scope=sc)
                AS = IU
            with ExitStack() as sc:
                ybhi = mb("ybhi", [P, HT, T], F32R, scope=sc)
                yblo = mb("yblo", [P, HT, T], F32R, scope=sc)
                pa = mb("pa", [P, 2, T], scope=sc)
                mg = mb("mg", [P, KD, T], scope=sc)
                mhi = mb("mhi", [P, KD, T], F32R, scope=sc)
                mlo = mb("mlo", [P, KD, T], F32R, scope=sc)

        yy = r
        gate_w = [A["ffn1_gate"][0].rearrange("(c p) f -> p c f", p=P),
                  A["ffn2_gate"][0].rearrange("(c p) f -> p c f", p=P)]
        up_w = [A["ffn1_up"][0].rearrange("(c p) f -> p c f", p=P),
                A["ffn2_up"][0].rearrange("(c p) f -> p c f", p=P)]
        down_w = [A["ffn1_down"][0].rearrange("(c p) f -> p c f", p=P),
                  A["ffn2_down"][0].rearrange("(c p) f -> p c f", p=P)]
        w_in = A["w_in"][0].rearrange("(c p) f -> p c f", p=P)
        proj_w = [A["proj_a"][0].rearrange("(c p) f -> p c f", p=P),
                  A["proj_b"][0].rearrange("(c p) f -> p c f", p=P)]
        w_out = A["w_out"][0].rearrange("(c p) f -> p c f", p=P)
        FFN = ((0, N_FFN1, N_DOWN1), (1, N_FFN2, N_DOWN2))
        NG = FF // W

        block = ctx.enter_context(nc.Block())

        @block.sync
        def _(sp):
            def load(n, half, slot, src, kts=KD, first=0):
                if not isinstance(n, int) or n >= 2:
                    sp.wait_ge(sg["lo_ready"], n - 1)
                sp.dma_start(raw[slot][:, first:first + kts], src).then_inc(w_landed[slot], 16)

            sp.dma_start(x_tok[:], A["x"][0].rearrange("(j p) d -> p j d", p=P)).then_inc(sg["x_in"], 16)
            sp.dma_start(cst[:], consts).then_inc(sg["const_in"], 16)

            for f, base, down in FFN:
                load(base, base // 2, 0, gate_w[f][:, :, 0:W])
                load(base + 1, base // 2, 1, up_w[f][:, :, 0:W])
                with sp.Fori(1, NG) as i:
                    load(2 * i + base, None, 0, gate_w[f][:, :, bass.ts(i, W)])
                    load(2 * i + base + 1, None, 1, up_w[f][:, :, bass.ts(i, W)])
                with sp.Fori(0, D // W // 2) as jp:
                    for t in range(6):
                        k0 = sum(KS[:t % 3])
                        load(6 * jp + (down + t), None, t % 2,
                             down_w[f][:, k0:k0 + KS[t % 3], bass.ds(jp * (2 * W) + (t // 3) * W, W)], KS[t % 3])
                if f == 0:
                    with sp.Fori(0, 3 * WM // W // 2) as i:
                        for s in range(2):
                            load(2 * i + N_RKV + s, None, s,
                                 w_in[:, :, bass.ds(i * (2 * W) + (3 * WM + s * W), W)])
                    with sp.Fori(0, 3 * WM // W // 2) as i:
                        for s in range(2):
                            load(2 * i + N_QK + s, None, s, w_in[:, :, bass.ds(i * (2 * W) + s * W, W)])
                    with sp.Fori(0, 2 * D // W // 2) as i:
                        for s in range(2):
                            load(2 * i + N_GATE + s, None, s,
                                 w_in[:, :, bass.ds(i * (2 * W) + (6 * WM + s * W), W)])
                    with sp.Fori(0, D // W // 2) as i:
                        for s in range(2):
                            cols = bass.ds(i * (2 * W) + s * W, W)
                            sp.wait_ge(sg["lo_ready"], 2 * i + N_PROJ + s - 1)
                            sp.dma_start(raw[s][:, 0:HT], proj_w[0][:, :, cols]).then_inc(w_landed[s], 16)
                            sp.dma_start(raw[s][:, HT:2 * HT], proj_w[1][:, :, cols]).then_inc(w_landed[s], 16)
                    with sp.Fori(0, D // W // 2) as i:
                        for s in range(2):
                            load(2 * i + N_OUT + s, None, s, w_out[:, :, bass.ds(i * (2 * W) + s * W, W)])
            sp.wait_ge(sg["final_copied"], 2)
            sp.wait_ge(sg["final_copied_act"], 2)
            sp.dma_start(out[0].rearrange("(j p) d -> p j d", p=P), out_tok[:]).then_inc(sg["out_stored"], 16)
            sp.wait_ge(sg["out_stored"], 16)

        def landings(n):
            return n // 2 + 1 + max(0, min(n // 2, N_OUT // 2 - 1) - N_PROJ // 2 + 1)

        EXTRA2 = landings(N_FFN2) - (N_FFN2 // 2 + 1)

        @block.gpsimd
        def _(pool):
            row = 0
            for name, (at, cols) in VECS.items():
                src = A[name]
                flat = {1: "d -> d", 2: "l d -> (l d)", 3: "l a d -> (l a d)"}[len(src.shape)]
                src = (src if len(src.shape) == 1 else src.rearrange(flat)).rearrange("(c p) -> c p", p=P)
                pool.dma_start(vec_rows[at:at + cols, :], src).then_inc(sg["vec_in"], 16)
            pool.dma_start(rel[:], A["rel_bias"]).then_inc(sg["vec_in"], 16)
            pool.wait_ge(sg["bias_row_sb"], 1)
            pool.dma_start(bias_dram, bias_sb[:]).then_inc(sg["bias_out"], 16)
            pool.wait_ge(sg["bias_out"], 16)
            pool.wait_ge(sg["x_ffn_odd"], 1 + KD // 2)
            for t, name in ((lwA, "w_lora_a"), (laA, "a_lora_a"), (lgA[:], "g_lora_a")):
                pool.dma_start(t, A[name][0].rearrange("(c p) n -> p c n", p=P)).then_inc(sg["lora_in"], 16)
            for t, name in ((lwB, "w_lora_b"), (laB, "a_lora_b")):
                pool.dma_start(t, A[name][0]).then_inc(sg["lora_in"], 16)
            pool.dma_start(lgB0, A["g_lora_b"][0][0:P]).then_inc(sg["lora_in"], 16)
            pool.dma_start(lgB1, A["g_lora_b"][0][P:GL]).then_inc(sg["lora_in"], 16)
            nc.gpsimd.memset(one[:], 0.0).then_inc(sg["pads_zero"], 1)
            nc.gpsimd.memset(dec[:, :, 0:1], 0.0).then_inc(sg["pads_zero"], 1)
            nc.gpsimd.memset(rkv[:, :, 0:1], 0.0).then_inc(sg["pads_zero"], 1)
            pool.wait_ge(sg["pads_zero"], 3)
            nc.gpsimd.memset(one[:, :, 0:1], 1.0).then_inc(sg["pads_zero"], 1)
            pool.wait_ge(sg["h_ready"], 2 * KD)
            nc.gpsimd.tensor_tensor(diff, h_m[:, :, 0:T], h_m[:, :, 1:T + 1], ALU.subtract).then_inc(sg["h_diff"], 1)
            pool.wait_ge(sg["h_diff"], 1)

            def mixed(which, dst, signal):
                for c in range(KD):
                    nc.gpsimd.tensor_scalar(dst[:, c], diff[:, c], v("mix_wag", which * KD + c), None,
                                            ALU.mult).then_inc(signal, 1)
                pool.wait_ge(signal, KD)
                nc.gpsimd.tensor_tensor(dst, dst, h_m[:, :, 1:T + 1], ALU.add).then_inc(signal, 1)

            mixed(0, xa0, sg["xw_ready"])
            mixed(1, xa1, sg["xa_ready"])
            pool.wait_ge(sg["tw_done"], 1)
            mixed(2, xa0, sg["xg_ready"])

            pool.wait_ge(sg["multiplied"], N_PROJ)
            pool.wait_ge(sg["xg_ready"], KD + 1)
            pool.dma_start(bias_w[:], bass.AP(bias_dram.tensor, 0, [[1, P], [384, H], [1, T]])).then_inc(sg["bias_in"], 16)

        @block.scalar
        def _(act):
            def hi(n, half, slot, kts=KD):
                act.wait_ge(w_landed[slot], 16 * half)
                if not isinstance(n, int) or n >= 2:
                    act.wait_ge(sg["multiplied"], n - 1)
                nc.scalar.activation(whi[slot][:, 0:kts], raw[slot][:, 0:kts], ACT.Copy).then_inc(sg["hi_ready"], 1)

            def hi_at(n, kts=KD):
                hi(n, landings(n), n % 2, kts)

            def norm(q, h, hview, split=None):
                for j in range(4):
                    nc.scalar.activation(hview[:, 2 * j:2 * j + 2], x[:, 2 * j:2 * j + 2],
                                         ACT.Square).then_inc(sg["squares"], 1)
                act.wait_ge(sg["mean_sq"], q + 1)
                nc.scalar.activation(rms[:], bank[4][:, 0:T], ACT.Sqrt,
                                     bias=cst[:, C_EPS:C_EPS + 1]).then_inc(sg["rms_ready"], 1)
                if split is not None:
                    for j in range(4):
                        act.wait_ge(sg["h_ready"], q * KD + 2 * j + 2)
                        nc.scalar.activation(split[:, 2 * j:2 * j + 2], hview[:, 2 * j:2 * j + 2],
                                             ACT.Copy).then_inc(sg["hhi_ready"], 1)

            def ffn(f, base, down):
                extra = EXTRA2 if f else 0
                g0 = NG * f

                def body(i, nexts):
                    act.wait_ge(sg["multiplied"], i * 2 + (base + 1))
                    if not isinstance(i, int) or i + g0 > 0:
                        act.wait_ge(sg["hid_prod"], i + g0)
                    nc.scalar.activation(silu[:], bank[0][:], ACT.Silu).then_inc(sg["silu_done"], 1)
                    nexts[0]()
                    nexts[1]()
                    act.wait_ge(sg["hid_prod"], i + (g0 + 1))
                    nc.scalar.activation(hid_hi[:, bass.ds(i * 2, 2)], prod[:], ACT.Copy).then_inc(sg["hid_hi"], 1)

                def nexts(i):
                    return [lambda s=s: hi(2 * i + (base + 2 + s), i + (base // 2 + 2 + extra), s) for s in range(2)]

                body(0, nexts(0))
                with act.Fori(1, NG - 1) as i:
                    body(i, nexts(i))
                body(NG - 1, [lambda s=s: hi(down + s, down // 2 + 1 + extra, s) for s in range(2)])

                def down_pair(jp, steps):
                    for t in range(2, 2 + steps):
                        hi(6 * jp + (down + t), 3 * jp + (down // 2 + t // 2 + 1 + extra), t % 2, KS[t % 3])

                if f == 0:
                    with act.Fori(0, 2) as jp:
                        down_pair(jp, 6)
                else:
                    down_pair(0, 6)
                    down_pair(1, 4)

            act.wait_ge(sg["vecT"], 1)
            nc.scalar.activation(vec[:], bank[7][:, 0:NVEC], ACT.Copy).then_inc(sg["vec_ready"], 1)
            for q in range(4):
                act.wait_ge(sg["x_T"], q + 1)
                nc.scalar.activation(x[:, 2 * q:2 * q + 2], bank[q][:].rearrange("p (c t) -> p c t", c=2),
                                     ACT.Copy).then_inc(sg["x_loaded"], 1)
            act.wait_ge(sg["x_loaded"], 4)
            norm(0, h_f, h_f, hhi_f)
            hi_at(0)
            hi_at(1)
            ffn(0, N_FFN1, N_DOWN1)

            act.wait_ge(sg["x_ffn_odd"], 1 + KD // 2)
            norm(1, h_m, h_m[:, :, 1:T + 1], hhi_m)

            def take(c, slot, dst, func=ACT.Copy, scale=1.0):
                act.wait_ge(sg["multiplied"], N_RKV + c + 1)
                nc.scalar.activation(dst, bank[slot][:].rearrange("p (m t) -> p m t", m=2), func,
                                     scale=scale).then_inc(sg["mix_taken"], 1)

            n = N_RKV
            act.wait_ge(sg["pads_zero"], 4)
            for c in range(6):
                take(c, c % 2, rkv[:, 2 * c:2 * c + 2, 1:T + 1])
                hi_at(n + c + 2)
            act.wait_ge(sg["tw_done"], 1)
            nc.scalar.activation(tws[:], bank[2][0:DL, 0:T], ACT.Tanh).then_inc(sg["tw_ready"], 1)
            act.wait_ge(sg["ta_done"], 1)
            nc.scalar.activation(tas[:], bank[3][0:AL, 0:T], ACT.Copy).then_inc(sg["ta_ready"], 1)
            act.wait_ge(sg["z_done"], 1)
            for j in range(HT):
                nc.scalar.activation(tmp[:, j], bank[6 + j // 2][:, (j % 2) * T:(j % 2 + 1) * T], ACT.Sigmoid,
                                     bias=v("w0", j)).then_inc(sg["sig_w"], 1)
            act.wait_ge(sg["a_done"], 1)
            for j in range(HT):
                nc.scalar.activation(aa[:, j], bank[2 + j // 2][:, (j % 2) * T:(j % 2 + 1) * T], ACT.Sigmoid,
                                     bias=v("a0", j)).then_inc(sg["a_ready"], 1)
            act.wait_ge(sg["sig_w"], HT)
            nc.scalar.activation(dec[:, :, 1:C + 1], tmp[:].rearrange("p j (q c) -> p (j q) c", c=C), ACT.Exp,
                                 scale=-EXP_HALF).then_inc(sg["decay_ready"], 1)
            for c in range(6, 20):
                n = N_RKV + c
                if c < 10:
                    take(c, c % 2, qk[:, 2 * (c - 6):2 * (c - 6) + 2], scale=HD ** -0.5 if c < 8 else 1.0)
                elif c < 12:
                    take(c, c % 2, va[:, :, (c - 10) * W:(c - 9) * W])
                else:
                    take(c, c % 2, gates[:, 2 * (c - 12):2 * (c - 12) + 2], ACT.Sigmoid)
                hi_at(n + 2)
                if c == 7:
                    act.wait_ge(sg["kk_sq_in"], 1)
                    act.wait_ge(sg["decay_ready"], 1)
                    nc.scalar.activation(tmp[:], kkn[:], ACT.Square).then_inc(sg["kk_sq"], 1)
                if c == 8:
                    act.wait_ge(sg["tg_done"], 1)
                    nc.scalar.activation(tg0[:], bank[4][:, 0:T], ACT.Sigmoid).then_inc(sg["tg_ready"], 1)
                    nc.scalar.activation(tg1[:], bank[5][0:GL - P, 0:T], ACT.Sigmoid).then_inc(sg["tg_ready"], 1)
                if c == 9:
                    act.wait_ge(sg["kk_ss"], 1)
                    for j in range(2):
                        nc.scalar.activation(tmp[:, 2 * j:2 * j + 2],
                                             bank[2 + j][:].rearrange("p (m t) -> p m t", m=2),
                                             ACT.Sqrt).then_inc(sg["kk_norm"], 1)
                if c == 10:
                    act.wait_ge(sg["g_done"], 1)
                    for j in range(2):
                        nc.scalar.activation(gg[:, 2 * j:2 * j + 2],
                                             bank[4 + j][:].rearrange("p (m t) -> p m t", m=2),
                                             ACT.Copy).then_inc(sg["g_ready"], 1)

            act.wait_ge(sg["bias_flip"], 1)
            for q in range(4):
                nc.scalar.activation(bias[:, 2 * q:2 * q + 2], bank[2 + q][:].rearrange("p (h t) -> p h t", h=2),
                                     ACT.Copy).then_inc(sg["bias_ready"], 1)
            for i in range(H + 2):
                if i < H:
                    act.wait_ge(sg["negmax"], i + 1)
                    for q, (lo_, hi_) in enumerate(((0, 2 * P), (2 * P, 3 * P))):
                        nc.scalar.activation(lg[:, i % 2, lo_:hi_], lg[:, i % 2, lo_:hi_], ACT.Exp,
                                             bias=stat[:, i, 2 + q:3 + q],
                                             accum_out=stat[:, i, 4 + q:5 + q]).then_inc(sg["exp_done"], 1)
                if 1 <= i <= H:
                    act.wait_ge(sg["pt_done"], i)
                    if i >= 3:
                        act.wait_ge(sg["pv_done"], i - 2)
                    nc.scalar.activation(pt[:, (i - 1) % 2], bank[2 + (i - 1) % 2][:, 0:3 * P],
                                         ACT.Copy).then_inc(sg["pt_ready"], 1)
                if i >= 2 and i % 2 == 1:
                    act.wait_ge(sg["pv_done"], i - 1)
                    j = (i - 3) // 2
                    nc.scalar.activation(yahi[:, j], bank[4 + j % 2][:, 0:T], ACT.Copy).then_inc(sg["ya_hi"], 1)

            for q in range(4):
                act.wait_ge(sg["vt_done"], 2 * q + 1)
                arr = (vt, None, bct, kct)[q]
                dst = AX[:, 0, :, 0:HD] if arr is None else arr[:, 0].rearrange("p (h n) -> p h n", n=HD)
                nc.scalar.activation(dst, bank[0][:].rearrange("p (h n) -> p h n", n=HD),
                                     ACT.Copy).then_inc(sg["vt_ready"], 1)
            for J in range(2):
                for g in range(2):
                    hs = slice(4 * g, 4 * g + 4)
                    act.wait_ge(sg["t2_done"], 2 * J + g + 1)
                    nc.scalar.activation(TT[:, hs], bank[6 + g][:].rearrange("p (h n) -> p h n", n=P),
                                         ACT.Copy).then_inc(sg["t2_ready"], 1)
                for lev in range(5):
                    for g in range(2):
                        hs = slice(4 * g, 4 * g + 4)
                        act.wait_ge(sg["level_done"], J * 10 + lev * 2 + g + 1)
                        nc.scalar.activation(G[:, hs], bank[6 + g][:].rearrange("p (h n) -> p h n", n=P),
                                             ACT.Copy).then_inc(sg["invT_ready"], 1)
                for g in range(2):
                    act.wait_ge(sg["as_done"], 2 * J + g + 1)
                    nc.scalar.activation(AS[:, 4 * g:4 * g + 4], bank[2 + g][:].rearrange("p (h n) -> p h n", n=P),
                                         ACT.Copy).then_inc(sg["as_ready"], 1)
                act.wait_ge(sg["y_done"], J + 1)
                for b in range(2):
                    nc.scalar.activation(yy[64 * b:64 * b + 64, :, J * P:(J + 1) * P],
                                         bank[b][64 * b:64 * b + 64, :].rearrange("p (j t) -> p j t", t=P),
                                         ACT.Copy).then_inc(sg["y_ready"], 1)
            act.wait_ge(sg["gdiff"], 2)
            nc.scalar.activation(tmp[:], yy[:], ACT.Square).then_inc(sg["gsq"], 1)
            act.wait_ge(sg["gvar"], 1)
            for j in range(2):
                nc.scalar.activation(tmp[:, 2 * j:2 * j + 2], bank[4 + j][:].rearrange("p (m t) -> p m t", m=2),
                                     ACT.Sqrt, bias=cst[:, C_EPS + 1:C_EPS + 2]).then_inc(sg["gstd"], 1)
            act.wait_ge(sg["yb_ready"], 1)
            nc.scalar.activation(ybhi[:], kt[:], ACT.Copy).then_inc(sg["yb_hi"], 1)
            for c in range(4):
                act.wait_ge(sg["merged"], c + 1)
                nc.scalar.activation(mhi[:, 2 * c:2 * c + 2], mg[:, 2 * c:2 * c + 2], ACT.Copy).then_inc(sg["m_hi"], 1)
                hi_at(N_PROJ + c + 2)
            for c in range(4):
                hi_at(N_OUT + c + 2)
            act.wait_ge(sg["x_mix"], 4)
            norm(2, h_f, h_f, hhi_f)
            ffn(1, N_FFN2, N_DOWN2)
            act.wait_ge(sg["x_ffn_odd"], 1 + KD)
            norm(3, h_f, h_f)
            for q in (1, 3):
                act.wait_ge(sg["final_T"], q + 1)
                nc.scalar.activation(out_tok[:, q // 2, (q % 2) * 512:(q % 2 + 1) * 512], bank[q][:],
                                     ACT.Copy).then_inc(sg["final_copied_act"], 1)

        @block.vector
        def _(dve):
            chain = [0]

            def link(ins):
                chain[0] += 1
                ins.then_inc(sg["dve_chain"], 1)
                dve.wait_ge(sg["dve_chain"], chain[0])

            def lo(n, slot, kts=KD):
                dve.wait_ge(sg["hi_ready"], n + 1)
                nc.vector.tensor_tensor(wlo[slot][:, 0:kts], raw[slot][:, 0:kts],
                                        whi[slot][:, 0:kts].bitcast(F32), ALU.subtract).then_inc(sg["lo_ready"], 1)

            def norm(q, gain, hview, split=None):
                dve.wait_ge(sg["rms_ready"], q + 1)
                link(nc.vector.reciprocal(rstd[:], rms[:]))
                for c in range(KD):
                    nc.vector.scalar_tensor_tensor(out=hview[:, c], in0=x[:, c], scalar=v(gain, c), in1=rstd[:],
                                                   op0=ALU.mult, op1=ALU.mult).then_inc(sg["h_ready"], 1)
                if split is not None:
                    for j in range(4):
                        dve.wait_ge(sg["hhi_ready"], 4 * q + j + 1)
                        nc.vector.tensor_tensor(split[1][:, 2 * j:2 * j + 2], hview[:, 2 * j:2 * j + 2],
                                                split[0][:, 2 * j:2 * j + 2].bitcast(F32),
                                                ALU.subtract).then_inc(sg["hlo_ready"], 1)

            def ffn(f, base, down):
                g0 = NG * f

                def body(i, nexts):
                    nexts[0]()
                    dve.wait_ge(sg["multiplied"], i * 2 + (base + 2))
                    dve.wait_ge(sg["silu_done"], i + (g0 + 1))
                    if not isinstance(i, int) or i + g0 > 0:
                        dve.wait_ge(sg["hid_lo"], i + g0)
                    nc.vector.tensor_tensor(prod[:], silu[:], bank[1][:].rearrange("p (m t) -> p m t", m=2),
                                            ALU.mult).then_inc(sg["hid_prod"], 1)
                    nexts[1]()
                    dve.wait_ge(sg["hid_hi"], i + (g0 + 1))
                    nc.vector.tensor_tensor(hid_lo[:, bass.ds(i * 2, 2)], prod[:],
                                            hid_hi[:, bass.ds(i * 2, 2)].bitcast(F32),
                                            ALU.subtract).then_inc(sg["hid_lo"], 1)

                def nexts(i):
                    return [lambda s=s: lo(2 * i + (base + 2 + s), s) for s in range(2)]

                body(0, nexts(0))
                with dve.Fori(1, NG - 1) as i:
                    body(i, nexts(i))
                body(NG - 1, [lambda s=s: lo(down + s, s) for s in range(2)])

                def add_down(jp, half, m):
                    if m == 0:
                        dve.wait_ge(sg["down_first"], 2 * jp + (half + f * (D // W) + 1))
                    else:
                        dve.wait_ge(sg["multiplied"], 6 * jp + (down + 3 * half + 3))
                    xt = x[:, bass.ds(4 * jp + (2 * half + m), 1)].rearrange("p a t -> p (a t)")
                    nc.vector.scalar_tensor_tensor(out=xt, in0=bank[2 + m][:, 0:T], scalar=0.5, in1=xt,
                                                   op0=ALU.mult, op1=ALU.add)\
                        .then_inc((sg["x_ffn_even"], sg["x_ffn_odd"])[m], 1)

                def down_pair(jp, steps):
                    for t in range(6):
                        if t < steps:
                            lo(6 * jp + (down + t + 2), t % 2, KS[(t + 2) % 3])
                        if t % 3 == 1:
                            add_down(jp, t // 3, 0)
                            add_down(jp, t // 3, 1)

                if f == 0:
                    with dve.Fori(0, 2) as jp:
                        down_pair(jp, 6)
                else:
                    down_pair(0, 6)
                    down_pair(1, 4)

            nc.vector.memset(idle[:, 0:1], 0.0).then_inc(sg["x_ffn_even"], 1)
            nc.vector.memset(idle[:, 1:2], 0.0).then_inc(sg["x_ffn_odd"], 1)
            dve.wait_ge(sg["bias_row"], 1)
            nc.vector.tensor_tensor(bias_sb[:], bank[6][0:H, 0:384], cst[0:H, C_NEG:C_NEG + 384],
                                    ALU.add).then_inc(sg["bias_row_sb"], 1)
            dve.wait_ge(sg["vec_ready"], 1)
            norm(0, "norm_ffn1", h_f, (hhi_f, hlo_f))
            lo(0, 0)
            lo(1, 1)
            ffn(0, N_FFN1, N_DOWN1)
            dve.wait_ge(sg["x_ffn_odd"], 1 + KD // 2)
            link(nc.vector.memset(h_m[:, :, 0:1], 0.0))
            norm(1, "norm_mix", h_m[:, :, 1:T + 1], (hhi_m, hlo_m))

            def shift_mix(which, dst, chunk):
                dve.wait_ge(sg["mix_taken"], chunk)
                src = rkv[:, which * HT:(which + 1) * HT]
                link(nc.vector.tensor_tensor(kt[:], src[:, :, 0:T], src[:, :, 1:T + 1], ALU.subtract))
                for j in range(HT):
                    last = nc.vector.scalar_tensor_tensor(out=dst[:, j], in0=kt[:, j], scalar=v("mix_rkv", which * HT + j),
                                                          in1=src[:, j, 1:T + 1], op0=ALU.mult, op1=ALU.add)
                link(last)

            view = lambda t: t[:].rearrange("p j (q c) -> p (j q) c", c=C)
            bank2 = lambda i: bank[i][:].rearrange("p (m t) -> p m t", m=2)
            for c in range(20):
                lo(N_RKV + c + 2, c % 2)
                if c == 1:
                    shift_mix(0, r, 2)
                if c == 3:
                    shift_mix(1, k, 4)
                    for j in range(HT):
                        last = nc.vector.tensor_scalar(kkn[:, j], k[:, j], v("k_k", j), None, ALU.mult)
                    last.then_inc(sg["kk_sq_in"], 1)
                if c == 5:
                    shift_mix(2, vv, 6)
                if c == 6:
                    dve.wait_ge(sg["decay_ready"], 1)
                    dve.wait_ge(sg["pads_zero"], 4)
                    link(nc.vector.tensor_tensor_scan(run[:].rearrange("p a b -> p (a b)"),
                                                      dec[:].rearrange("p a b -> p (a b)"),
                                                      one[:].rearrange("p a b -> p (a b)"), 0.0,
                                                      ALU.mult, ALU.add))
                    link(nc.vector.reciprocal(inv_run, run_t))
                    dve.wait_ge(sg["a_ready"], HT)
                    for j in range(HT):
                        last = nc.vector.tensor_scalar(kt[:, j], aa[:, j], 1.0, v("k_a", j), ALU.subtract, ALU.mult)
                    link(last)
                    link(nc.vector.scalar_tensor_tensor(out=k[:], in0=kt[:], scalar=1.0, in1=k[:],
                                                        op0=ALU.add, op1=ALU.mult))
                if c == 7:
                    nc.vector.tensor_tensor(view(kt), view(k), inv_run, ALU.mult)
                    dve.wait_ge(sg["xg_ready"], KD + 1)
                    link(nc.vector.tensor_tensor(AR[:, 1].rearrange("p j (q c) -> p (j q) c", c=C), view(r), run_t,
                                                 ALU.mult))
                    nc.vector.tensor_tensor(dpc, cst[:, C_SUI:C_SUI + C].unsqueeze(1).to_broadcast([P, HT * NCH, C]),
                                            run_end.to_broadcast([P, HT * NCH, C]), ALU.mult).then_inc(sg["ab_ready"], 1)
                if c == 10:
                    dve.wait_ge(sg["kk_norm"], 2)
                    link(nc.vector.tensor_scalar(tmp[:], tmp[:], 1e-12, None, ALU.max))
                    link(nc.vector.reciprocal(tmp[:], tmp[:]))
                    link(nc.vector.tensor_tensor(kkn[:], kkn[:], tmp[:], ALU.mult))
                    link(nc.vector.tensor_tensor(aa[:], kkn[:], aa[:], ALU.mult))
                if c == 11:
                    link(nc.vector.tensor_tensor(view(aa), view(aa), inv_run, ALU.mult))
                    nc.vector.scalar_tensor_tensor(out=AR[:, 0].rearrange("p j (q c) -> p (j q) c", c=C),
                                                   in0=view(kkn), scalar=-1.0, in1=run_before,
                                                   op0=ALU.mult, op1=ALU.mult).then_inc(sg["ab_ready"], 1)
                if c == 12:
                    dve.wait_ge(sg["ab_ready"], 2)
                    nc.vector.tensor_tensor(view(bc), view(aa), run_end.to_broadcast([P, HT * NCH, C]),
                                            ALU.mult).then_inc(sg["kc_ready"], 1)
                    nc.vector.tensor_tensor(view(kc), view(kt), run_end.to_broadcast([P, HT * NCH, C]),
                                            ALU.mult).then_inc(sg["kc_ready"], 1)
                if c == 14:
                    for j in range(HT):
                        last = nc.vector.scalar_tensor_tensor(out=r[:, j], in0=r[:, j], scalar=v("r_k", j), in1=k[:, j],
                                                              op0=ALU.mult, op1=ALU.mult)
                    last.then_inc(sg["rkk_ready"], 1)
                if c == 17:
                    dve.wait_ge(sg["rkk_sum"], 1)
                    for j in range(2):
                        nc.vector.tensor_tensor(k[:, 2 * j:2 * j + 2], vv[:, 2 * j:2 * j + 2], bank2(2 + j),
                                                ALU.mult).then_inc(sg["bonus_done"], 1)

            dve.wait_ge(sg["bias_ready"], 4)
            for i in range(H + 1):
                if i < H:
                    dve.wait_ge(sg["s_done"], i + 1)
                    if i >= 2:
                        dve.wait_ge(sg["pt_done"], i - 1)
                    s = bank[i % 2]
                    nc.vector.tensor_tensor(lg[:, i % 2, 0:2 * P], s[:, 0:2 * P], bias[:, i, 0:2 * P],
                                            ALU.add).then_inc(sg["logits"], 1)
                    nc.vector.tensor_tensor(lg[:, i % 2, 2 * P:3 * P], s[:, 2 * P:3 * P], bias[:, i, P:2 * P],
                                            ALU.add).then_inc(sg["logits"], 1)
                    dve.wait_ge(sg["logits"], 2 * i + 1)
                    nc.vector.reduce_max(stat[:, i, 0:1], lg[:, i % 2, 0:2 * P], mybir.AxisListType.X)
                    dve.wait_ge(sg["logits"], 2 * i + 2)
                    link(nc.vector.reduce_max(stat[:, i, 1:2], lg[:, i % 2, 2 * P:3 * P], mybir.AxisListType.X))
                    nc.vector.tensor_scalar(stat[:, i, 2:4], stat[:, i, 0:2], -1.0, None,
                                            ALU.mult).then_inc(sg["negmax"], 1)
                if i >= 1:
                    h = i - 1
                    dve.wait_ge(sg["exp_done"], 2 * h + 2)
                    link(nc.vector.reciprocal(stat[:, h, 6:8], stat[:, h, 4:6]))
                    nc.vector.tensor_scalar(lg[:, h % 2, 0:2 * P], lg[:, h % 2, 0:2 * P], stat[:, h, 6:7], None,
                                            ALU.mult).then_inc(sg["prob_ready"], 1)
                    nc.vector.tensor_scalar(lg[:, h % 2, 2 * P:3 * P], lg[:, h % 2, 2 * P:3 * P], stat[:, h, 7:8],
                                            None, ALU.mult).then_inc(sg["prob_ready"], 1)
                if i >= 4 and i % 2 == 0:
                    j = (i - 4) // 2
                    dve.wait_ge(sg["ya_hi"], j + 1)
                    nc.vector.tensor_tensor(yalo[:, j], bank[4 + j % 2][:, 0:T], yahi[:, j].bitcast(F32),
                                            ALU.subtract).then_inc(sg["ya_lo"], 1)
            dve.wait_ge(sg["ya_hi"], 4)
            nc.vector.tensor_tensor(yalo[:, 3], bank[5][:, 0:T], yahi[:, 3].bitcast(F32),
                                    ALU.subtract).then_inc(sg["ya_lo"], 1)

            for q in range(4):
                dve.wait_ge(sg["vt_done"], 2 * q + 2)
                arr = (vt, None, bct, kct)[q]
                dst = AX[:, 1, :, 0:HD] if arr is None else arr[:, 1].rearrange("p (h n) -> p h n", n=HD)
                nc.vector.tensor_copy(dst, bank[1][:].rearrange("p (h n) -> p h n", n=HD)).then_inc(sg["tok_ready"], 1)
            eye4 = ident.unsqueeze(1).to_broadcast([P, 4, P])
            for J in range(2):
                def mask(name, n):
                    return mat(name).unsqueeze(1).to_broadcast([P, n, P])

                for q in range(8):
                    dve.wait_ge(sg["pair_done"], 8 * J + q + 1)
                    par, pos, dst = q % 2, q // 2 % 2, (NR, KK)[q // 4]
                    heads = dst[:, 4 * pos + par:4 * pos + par + 3:2]
                    src = bank[2 + q % 4][:].rearrange("p (h a t) -> p h a t", h=2, a=2)
                    nc.vector.tensor_tensor(heads[:, :, 0], src[:, :, 0], mask("low_a", 2), ALU.mult)
                    nc.vector.tensor_tensor(heads[:, :, 1], src[:, :, 1], mask("low_r", 2),
                                            ALU.mult).then_inc(sg["pair_ready"], 1)
                    if q == 3:
                        dve.wait_ge(sg["pair_ready"], 8 * J + 4)
                        for g in range(2):
                            hs = slice(4 * g, 4 * g + 4)
                            nc.vector.tensor_tensor(NR[:, hs, 0], NR[:, hs, 0], eye4, ALU.add).then_inc(sg["n_ready"], 1)
                        for g in range(2):
                            hs = slice(4 * g, 4 * g + 4)
                            dve.wait_ge(sg["n_ready"], 2 * J + g + 1)
                            nc.vector.tensor_tensor(G[:, hs], NR[:, hs, 0], mask("g2", 4), ALU.mult).then_inc(sg["g2_ready"], 1)
                for lev in range(5):
                    for g in range(2):
                        hs = slice(4 * g, 4 * g + 4)
                        dve.wait_ge(sg["u_done"], J * 10 + lev * 2 + g + 1)
                        nc.vector.tensor_tensor(IU[:, hs], bank[4 + g][:].rearrange("p (h n) -> p h n", n=P),
                                                mask(f"lev{2 << lev}", 4), ALU.mult).then_inc(sg["iu_ready"], 1)
                    if lev < 4:
                        for g in range(2):
                            hs = slice(4 * g, 4 * g + 4)
                            dve.wait_ge(sg["level_done"], J * 10 + lev * 2 + g + 1)
                            nc.vector.tensor_copy(TT[:, hs], bank[2 + g][:].rearrange("p (h n) -> p h n", n=P))\
                                .then_inc(sg["inv_ready"], 1)
                dve.wait_ge(sg["x1_done"], J + 1)
                nc.vector.tensor_copy(AX[:, J, :, HD:P], bank[4][:].rearrange("p (h n) -> p h n", n=HD))\
                    .then_inc(sg["tok_ready"], 1)
                dve.wait_ge(sg["rh_done"], J + 1)
                rs = AR[:, 1, :, J * P:(J + 1) * P]
                nc.vector.tensor_tensor(rs, bank[5][:].rearrange("p (j t) -> p j t", t=P), rs, ALU.add)\
                    .then_inc(sg["rh_ready"], 1)
                dve.wait_ge(sg["phi_done"], J + 1)
                for c in range(2):
                    src = bank[6 + c][:].rearrange("p (a j n) -> p a j n", a=2, j=HT)
                    ends = dpc.rearrange("p (j q) n -> p j q n", q=NCH)[:, :, 2 * J + c]
                    nc.vector.tensor_tensor(phi[:, c, 0], src[:, 0], ends, ALU.add)
                    last = nc.vector.tensor_copy(phi[:, c, 1], src[:, 1])
                    if J == 0 and c == 0:
                        nc.vector.tensor_copy(state[:, 1], src[:, 1])
                last.then_inc(sg["phi_ready"], 1)
                dve.wait_ge(sg["phi_ready"], J + 1)
                for c in range(2):
                    q = 2 * J + c
                    if 1 <= q <= 2:
                        dve.wait_ge(sg["st_done"], q)
                        for b in range(2):
                            bs = slice(64 * b, 64 * b + 64)
                            nc.vector.tensor_tensor(state[bs, q + 1], phi[bs, c, 1],
                                                    bank[2 + b][bs, 0:HT * C].rearrange("p (j n) -> p j n", n=C),
                                                    ALU.add).then_inc(sg["st_ready"], 1)
            dve.wait_ge(sg["gmean"], 1)
            dve.wait_ge(sg["y_ready"], 4)
            for j in range(2):
                nc.vector.tensor_tensor(yy[:, 2 * j:2 * j + 2], yy[:, 2 * j:2 * j + 2], bank2(2 + j),
                                        ALU.subtract).then_inc(sg["gdiff"], 1)
            dve.wait_ge(sg["gstd"], 2)
            link(nc.vector.reciprocal(tmp[:], tmp[:]))
            link(nc.vector.tensor_tensor(yy[:], yy[:], tmp[:], ALU.mult))
            for j in range(HT):
                last = nc.vector.tensor_scalar(yy[:, j], yy[:, j], v("ln_x_w", j), v("ln_x_b", j), ALU.mult, ALU.add)
            link(last)
            dve.wait_ge(sg["bonus_done"], 2)
            link(nc.vector.tensor_tensor(yy[:], yy[:], k[:], ALU.add))
            dve.wait_ge(sg["g_ready"], 2)
            nc.vector.tensor_tensor(kt[:], yy[:], gg[:], ALU.mult).then_inc(sg["yb_ready"], 1)
            dve.wait_ge(sg["yb_hi"], 1)
            nc.vector.tensor_tensor(yblo[:], kt[:], ybhi[:].bitcast(F32), ALU.subtract).then_inc(sg["yb_lo"], 1)
            for c in range(4):
                dve.wait_ge(sg["multiplied"], N_PROJ + c + 1)
                b = 2 * (c % 2)
                link(nc.vector.tensor_tensor(pa[:], gates[:, 2 * c:2 * c + 2], bank2(b), ALU.mult))
                link(nc.vector.tensor_tensor(mg[:, 2 * c:2 * c + 2], gates[:, KD + 2 * c:KD + 2 * c + 2], bank2(b + 1),
                                             ALU.mult))
                nc.vector.tensor_tensor(mg[:, 2 * c:2 * c + 2], mg[:, 2 * c:2 * c + 2], pa[:],
                                        ALU.add).then_inc(sg["merged"], 1)
                dve.wait_ge(sg["m_hi"], c + 1)
                nc.vector.tensor_tensor(mlo[:, 2 * c:2 * c + 2], mg[:, 2 * c:2 * c + 2],
                                        mhi[:, 2 * c:2 * c + 2].bitcast(F32), ALU.subtract).then_inc(sg["m_lo"], 1)
                lo(N_PROJ + c + 2, c % 2)
            for c in range(4):
                lo(N_OUT + c + 2, c % 2)
                dve.wait_ge(sg["multiplied"], N_OUT + c + 1)
                nc.vector.tensor_tensor(x[:, 2 * c:2 * c + 2], x[:, 2 * c:2 * c + 2], bank2(4 + c % 2),
                                        ALU.add).then_inc(sg["x_mix"], 1)
            dve.wait_ge(sg["x_mix"], 4)
            norm(2, "norm_ffn2", h_f, (hhi_f, hlo_f))
            ffn(1, N_FFN2, N_DOWN2)
            dve.wait_ge(sg["x_ffn_odd"], 1 + KD)
            norm(3, "norm_final", h_f)
            for q in (0, 2):
                dve.wait_ge(sg["final_T"], q + 1)
                nc.vector.tensor_copy(out_tok[:, q // 2, (q % 2) * 512:(q % 2 + 1) * 512], bank[q][:])\
                    .then_inc(sg["final_copied"], 1)

        @block.tensor
        def _(pe):
            mm = nc.tensor.matmul

            def part(dst, lhsT, rhs, start=False):
                return mm(dst, lhsT, rhs, start=start, stop=True, skip_group_check=True)

            def three(dst, slot, k_, cols, xh, xl, start, stop):
                mm(dst, whi[slot][:, k_, cols], xl, start=start, stop=False)
                mm(dst, wlo[slot][:, k_, cols], xh, start=False, stop=False)
                return mm(dst, whi[slot][:, k_, cols], xh, start=False, stop=stop)

            def columns(dst, slot, hh, hl, q=None, ks=range(KD)):
                for m in range(2):
                    for c in ks:
                        if q is not None and m == 0 and c % 2 == 0:
                            pe.wait_ge(sg["hlo_ready"], 4 * q + c // 2 + 1)
                        last = three(dst[:, m * T:(m + 1) * T], slot, c, slice(m * P, (m + 1) * P),
                                     hh[:, c], hl[:, c], c == ks[0], c == ks[-1])
                return last

            def norm(q, hview):
                for c in range(KD):
                    if c % 2 == 0:
                        pe.wait_ge(sg["squares"], 4 * q + c // 2 + 1)
                    last = mm(bank[4][:, 0:T], mat("mean_d"), hview[:, c], start=c == 0, stop=c == KD - 1)
                last.then_inc(sg["mean_sq"], 1)

            def ffn(f, base, down, q):
                g0 = NG * f

                def chunk(i, s, q_=None):
                    pe.wait_ge(sg["lo_ready"], 2 * i + (base + 1 + s))
                    if not isinstance(i, int) or i + g0 > 0:
                        pe.wait_ge((sg["silu_done"], sg["hid_prod"])[s], i + g0)
                    columns(bank[s], s, hhi_f, hlo_f, q_).then_inc(sg["multiplied"], 1)

                chunk(0, 0, q)
                chunk(0, 1)
                with pe.Fori(1, NG) as i:
                    chunk(i, 0)
                    chunk(i, 1)

                with pe.Fori(0, D // W // 2) as jp:
                    for t in range(6):
                        part_, s, half = t % 3, t % 2, t // 3
                        k0 = sum(KS[:part_])
                        pe.wait_ge(sg["lo_ready"], 6 * jp + (down + t + 1))
                        pe.wait_ge(sg["hid_lo"], g0 + (k0 + KS[part_]) // 2)
                        for m in range(2):
                            if part_ == 0:
                                pe.wait_ge((sg["x_ffn_even"], sg["x_ffn_odd"])[m], 2 * jp + (f * (D // W) + half + 1))
                            for c in range(KS[part_]):
                                last = three(bank[2 + m][:, 0:T], s, c, slice(m * P, (m + 1) * P),
                                             hid_hi[:, k0 + c], hid_lo[:, k0 + c],
                                             k0 + c == 0, k0 + c == FT - 1)
                            if part_ == 2 and m == 0:
                                last.then_inc(sg["down_first"], 1)
                        last.then_inc(sg["multiplied"], 1)

            pe.wait_ge(sg["const_in"], 16)
            pe.wait_ge(sg["x_in"], 16)
            for q in range(4):
                for c in range(2):
                    for j in range(2):
                        last = nc.tensor.transpose(bank[q][:, c * T + j * P:c * T + (j + 1) * P],
                                                   x_tok[:, j, (2 * q + c) * P:(2 * q + c + 1) * P], ident)
                last.then_inc(sg["x_T"], 1)
            pe.wait_ge(sg["vec_in"], 16 * (len(VECS) + 1))
            nc.tensor.transpose(bank[7][:, 0:NVEC], vec_rows[:], ident[0:NVEC, 0:NVEC]).then_inc(sg["vecT"], 1)
            mm(bank[6][0:H, 0:384], rel[:], cst[0:NB, C_HOT:C_HOT + 384], start=True, stop=True)\
                .then_inc(sg["bias_row"], 1)
            norm(0, h_f)
            ffn(0, N_FFN1, N_DOWN1, 0)
            norm(1, h_m[:, :, 1:T + 1])

            def product(c, s, q=None):
                pe.wait_ge(sg["lo_ready"], N_RKV + c + 1)
                if not isinstance(c, int) or c >= 2:
                    pe.wait_ge(sg["mix_taken"], c - 1)
                columns(bank[s], s, hhi_m, hlo_m, q).then_inc(sg["multiplied"], 1)

            product(0, 0, 1)
            product(1, 1)
            with pe.Fori(2, 6, 2) as c:
                product(c, 0)
                product(c + 1, 1)

            def lora_in(dst, w, xs, rows):
                for c in range(KD):
                    last = mm(dst, w[:, c, rows], xs[:, c], start=c == 0, stop=c == KD - 1)
                return last

            pe.wait_ge(sg["lora_in"], 16 * 7)
            pe.wait_ge(sg["xw_ready"], KD + 1)
            lora_in(bank[2][0:DL, 0:T], lwA, xa0, slice(0, DL)).then_inc(sg["tw_done"], 1)
            pe.wait_ge(sg["xa_ready"], KD + 1)
            lora_in(bank[3][0:AL, 0:T], laA, xa1, slice(0, AL)).then_inc(sg["ta_done"], 1)
            pe.wait_ge(sg["tw_ready"], 1)
            for j in range(HT):
                last = part(bank[6 + j // 2][:, (j % 2) * T:(j % 2 + 1) * T], lwB[:, j * P:(j + 1) * P], tws[:],
                            True)
            last.then_inc(sg["z_done"], 1)
            pe.wait_ge(sg["ta_ready"], 1)
            for j in range(HT):
                last = part(bank[2 + j // 2][:, (j % 2) * T:(j % 2 + 1) * T], laB[:, j * P:(j + 1) * P], tas[:],
                            True)
            last.then_inc(sg["a_done"], 1)
            product(6, 0)
            product(7, 1)
            pe.wait_ge(sg["xg_ready"], KD + 1)
            lora_in(bank[4][:, 0:T], lgA, xa0, slice(0, P))
            lora_in(bank[5][0:GL - P, 0:T], lgA, xa0, slice(P, GL)).then_inc(sg["tg_done"], 1)
            product(8, 0)
            pe.wait_ge(sg["kk_sq"], 1)
            pe.wait_ge(sg["a_ready"], HT)
            for j in range(2):
                last = mm(bank[2 + j][:], mat("head_sum"), tmp[:, 2 * j:2 * j + 2], start=True, stop=True)
            last.then_inc(sg["kk_ss"], 1)
            product(9, 1)
            pe.wait_ge(sg["tg_ready"], 2)
            for j in range(HT):
                dst = bank[4 + j // 2][:, (j % 2) * T:(j % 2 + 1) * T]
                mm(dst, lgB0[:, j * P:(j + 1) * P], tg0[:], start=True, stop=False)
                last = mm(dst, lgB1[:, j * P:(j + 1) * P], tg1[:], start=False, stop=True)
            last.then_inc(sg["g_done"], 1)
            for c in range(10, 12):
                pe.wait_ge(sg["lo_ready"], N_RKV + c + 1)
                pe.wait_ge(sg["mix_taken"], c - 1)
                for j in range(2):
                    ts = slice(j * P, (j + 1) * P)
                    dst = bank[c % 2][:, j * T:(j + 1) * T]
                    for k_ in range(KD):
                        mm(dst, hlo_m[:, k_, ts], whi[c % 2][:, k_], start=k_ == 0, stop=False)
                        mm(dst, hhi_m[:, k_, ts], wlo[c % 2][:, k_], start=False, stop=False)
                        last = mm(dst, hhi_m[:, k_, ts], whi[c % 2][:, k_], start=False, stop=k_ == KD - 1)
                last.then_inc(sg["multiplied"], 1)
            with pe.Fori(12, 18, 2) as c:
                product(c, 0)
                product(c + 1, 1)
            pe.wait_ge(sg["rkk_ready"], 1)
            pe.wait_ge(sg["kk_norm"], 2)
            for j in range(2):
                last = mm(bank[2 + j][:], mat("head_sum"), r[:, 2 * j:2 * j + 2], start=True, stop=True)
            last.then_inc(sg["rkk_sum"], 1)
            product(18, 0)
            product(19, 1)

            pe.wait_ge(sg["bias_in"], 16)
            pe.wait_ge(sg["bonus_done"], 2)
            for q in range(4):
                last = mm(bank[2 + q][:], flip, bias_w[:, 2 * q:2 * q + 2], start=True, stop=True)
            last.then_inc(sg["bias_flip"], 1)
            pe.wait_ge(sg["mix_taken"], 20)
            pe.wait_ge(sg["bias_ready"], 4)
            for i in range(H + 2):
                if i < H:
                    j, bs = i // 2, slice(64 * (i % 2), 64 * (i % 2) + 64)
                    if i >= 2:
                        pe.wait_ge(sg["logits"], 2 * (i - 1))
                    part(bank[i % 2][:, 0:2 * P], qk[bs, j, P:2 * P], qk[bs, HT + j], True)
                    part(bank[i % 2][:, 2 * P:3 * P], qk[bs, j, 0:P], qk[bs, HT + j, 0:P])\
                        .then_inc(sg["s_done"], 1)
                if 1 <= i <= H:
                    h = i - 1
                    pe.wait_ge(sg["prob_ready"], 2 * (h + 1))
                    if h >= 2:
                        pe.wait_ge(sg["pt_ready"], h - 1)
                    b = bank[2 + h % 2]
                    nc.tensor.transpose(b[:, 0:P], lg[:, h % 2, 2 * P:3 * P], ident)
                    nc.tensor.transpose(b[:, P:2 * P], lg[:, h % 2, 0:P], ident)
                    nc.tensor.transpose(b[:, 2 * P:3 * P], lg[:, h % 2, P:2 * P], ident).then_inc(sg["pt_done"], 1)
                if i >= 2:
                    h = i - 2
                    j, bs = h // 2, slice(64 * (h % 2), 64 * (h % 2) + 64)
                    pe.wait_ge(sg["pt_ready"], h + 1)
                    if j >= 2:
                        pe.wait_ge(sg["ya_lo"], j - 1)
                    part(bank[4 + j % 2][bs, 0:T], va[:, 0, h * HD:(h + 1) * HD], pt[:, h % 2, 0:T], True)
                    part(bank[4 + j % 2][bs, P:T], va[:, 1, h * HD:(h + 1) * HD], pt[:, h % 2, T:3 * P])\
                        .then_inc(sg["pv_done"], 1)

            pe.wait_ge(sg["kc_ready"], 2)
            for q in range(4):
                for J in range(2):
                    if q:
                        pe.wait_ge((sg["vt_ready"], sg["tok_ready"])[J], q)
                    else:
                        pe.wait_ge(sg["logits"], 2 * H)
                    for j in range(HT):
                        src = (vv[:, j], AR[:, 0, j], bc[:, j], kc[:, j])[q]
                        last = nc.tensor.transpose(bank[J][:, j * P:(j + 1) * P], src[:, J * P:(J + 1) * P], ident)
                    last.then_inc(sg["vt_done"], 1)
            pe.wait_ge(sg["ya_lo"], HT)
            for J in range(2):
                sl = slice(J * P, (J + 1) * P)
                pe.wait_ge(sg["ab_ready"], 2)
                if J:
                    pe.wait_ge(sg["st_ready"], 2)
                for q in range(8):
                    par, pos = q % 2, q // 2 % 2
                    bs = slice(64 * par, 64 * par + 64)
                    if q >= 4:
                        pe.wait_ge(sg["pair_ready"], 8 * J + q - 3)
                    for t in range(2):
                        j = 2 * pos + t
                        last = part(bank[2 + q % 4][:, t * 2 * P:(t + 1) * 2 * P], (aa, kt)[q // 4][bs, j, sl],
                                    AR[bs, :, j, sl], t == 0)
                    last.then_inc(sg["pair_done"], 1)
                for g in range(2):
                    pe.wait_ge(sg["g2_ready"], 2 * J + g + 1)
                    for i in range(4):
                        last = nc.tensor.transpose(bank[6 + g][:, i * P:(i + 1) * P], G[:, 4 * g + i], ident)
                    last.then_inc(sg["t2_done"], 1)
                for lev in range(5):
                    for g in range(2):
                        if lev == 0:
                            pe.wait_ge(sg["t2_ready"], 2 * J + g + 1)
                            pe.wait_ge(sg["pair_ready"], 8 * J + 7 + g)
                        else:
                            pe.wait_ge(sg["inv_ready"], 8 * J + 2 * (lev - 1) + g + 1)
                        for i in range(4):
                            last = part(bank[4 + g][:, i * P:(i + 1) * P], NR[:, 4 * g + i, 0], TT[:, 4 * g + i],
                                        i == 0)
                        last.then_inc(sg["u_done"], 1)
                    for g in range(2):
                        pe.wait_ge(sg["iu_ready"], 10 * J + 2 * lev + g + 1)
                        if lev:
                            pe.wait_ge(sg["invT_ready"], 10 * J + 2 * (lev - 1) + g + 1)
                        if lev < 4:
                            for i in range(4):
                                part(bank[2 + g][:, i * P:(i + 1) * P], G[:, 4 * g + i], IU[:, 4 * g + i], i == 0)
                        for i in range(4):
                            last = part(bank[6 + g][:, i * P:(i + 1) * P], IU[:, 4 * g + i], G[:, 4 * g + i],
                                        i == 0)
                        last.then_inc(sg["level_done"], 1)
                for h in range(H):
                    last = part(bank[4][:, h * HD:(h + 1) * HD], KK[:, h, 0], vt[:, J, h * HD:(h + 1) * HD], h == 0)
                last.then_inc(sg["x1_done"], 1)
                pe.wait_ge(sg["tok_ready"], 5 + J)
                for g in range(2):
                    pe.wait_ge(sg["invT_ready"], 10 * J + 8 + g + 1)
                    for i in range(4):
                        last = part(bank[2 + g][:, i * P:(i + 1) * P], G[:, 4 * g + i], AX[:, J, 4 * g + i], i == 0)
                    last.then_inc(sg["as_done"], 1)
                pe.wait_ge(sg["as_ready"], 2 * J + 2)
                for h in range(H):
                    j, bs = h // 2, slice(64 * (h % 2), 64 * (h % 2) + 64)
                    last = part(bank[5][bs, j * P:(j + 1) * P], AS[:, h, 0:HD], NR[:, h, 1], j == 0)
                last.then_inc(sg["rh_done"], 1)
                for h in range(H):
                    j, bs, hc = h // 2, slice(64 * (h % 2), 64 * (h % 2) + 64), slice(h * HD, (h + 1) * HD)
                    for c in range(2):
                        cs = slice(64 * c, 64 * c + 64)
                        part(bank[6 + c][bs, j * C:(j + 1) * C], AS[cs, h, 0:HD], bct[cs, J, hc], j == 0)
                for h in range(H):
                    j, bs, hc = h // 2, slice(64 * (h % 2), 64 * (h % 2) + 64), slice(h * HD, (h + 1) * HD)
                    for c in range(2):
                        cs = slice(64 * c, 64 * c + 64)
                        psi = bank[6 + c][bs, (HT + j) * C:(HT + j + 1) * C]
                        part(psi, bct[cs, J, hc], AS[cs, h, HD:P])
                        last = part(psi, kct[cs, J, hc], vt[cs, J, hc])
                last.then_inc(sg["phi_done"], 1)
                if J:
                    pe.wait_ge(sg["y_ready"], 2)
                for h in range(H):
                    j, bs, hc = h // 2, slice(64 * (h % 2), 64 * (h % 2) + 64), slice(h * HD, (h + 1) * HD)
                    dst = bank[h % 2][bs, j * P:(j + 1) * P]
                    part(dst, AS[:, h, HD:P], NR[:, h, 1], j == 0)
                    part(dst, vt[:, J, hc], KK[:, h, 1])
                pe.wait_ge(sg["phi_ready"], J + 1)
                pe.wait_ge(sg["rh_ready"], J + 1)
                for c in range(2):
                    q = 2 * J + c
                    if q == 0:
                        continue
                    if q >= 2:
                        pe.wait_ge(sg["st_ready"], 2 * (q - 1))
                    if q < NCH - 1:
                        for h in range(H):
                            j, bs = h // 2, slice(64 * (h % 2), 64 * (h % 2) + 64)
                            last = part(bank[2 + h % 2][bs, j * C:(j + 1) * C], phi[bs, c, 0, j], state[bs, q, j],
                                        j == 0)
                        last.then_inc(sg["st_done"], 1)
                    for h in range(H):
                        j, bs = h // 2, slice(64 * (h % 2), 64 * (h % 2) + 64)
                        last = part(bank[h % 2][bs, j * P + c * C:j * P + (c + 1) * C], state[bs, q, j],
                                    AR[bs, 1, j, q * C:(q + 1) * C])
                last.then_inc(sg["y_done"], 1)
            pe.wait_ge(sg["y_ready"], 4)
            for j in range(2):
                last = mm(bank[2 + j][:], mat("head_mean"), yy[:, 2 * j:2 * j + 2], start=True, stop=True)
            last.then_inc(sg["gmean"], 1)
            pe.wait_ge(sg["gsq"], 1)
            for j in range(2):
                last = mm(bank[4 + j][:], mat("head_mean"), tmp[:, 2 * j:2 * j + 2], start=True, stop=True)
            last.then_inc(sg["gvar"], 1)
            for c in range(4):
                s = c % 2
                pe.wait_ge(sg["lo_ready"], N_PROJ + c + 1)
                if c >= 2:
                    pe.wait_ge(sg["merged"], c - 1)
                columns(bank[2 * s], s, yahi, yalo, ks=range(HT))
                if c == 0:
                    pe.wait_ge(sg["yb_lo"], 1)
                for m in range(2):
                    for j in range(HT):
                        last = three(bank[2 * s + 1][:, m * T:(m + 1) * T], s, HT + j, slice(m * P, (m + 1) * P),
                                     ybhi[:, j], yblo[:, j], j == 0, j == HT - 1)
                last.then_inc(sg["multiplied"], 1)
            pe.wait_ge(sg["m_lo"], 4)
            for c in range(4):
                pe.wait_ge(sg["lo_ready"], N_OUT + c + 1)
                if c >= 2:
                    pe.wait_ge(sg["x_mix"], c - 1)
                columns(bank[4 + c % 2], c % 2, mhi, mlo).then_inc(sg["multiplied"], 1)
            norm(2, h_f)
            ffn(1, N_FFN2, N_DOWN2, 2)
            norm(3, h_f)
            pe.wait_ge(sg["h_ready"], 4 * KD)
            for q in range(4):
                for i in range(4):
                    last = nc.tensor.transpose(bank[q][:, i * P:(i + 1) * P],
                                               h_f[:, 4 * (q % 2) + i, (q // 2) * P:(q // 2 + 1) * P], ident)
                last.then_inc(sg["final_T"], 1)


_INS = ("x", "rel_bias", "norm_ffn1", "ffn1_gate", "ffn1_up", "ffn1_down", "norm_mix", "w_in", "mix_rkv",
        "mix_wag", "w_lora_a", "w_lora_b", "w0", "a_lora_a", "a_lora_b", "a0", "g_lora_a", "g_lora_b", "k_k",
        "k_a", "r_k", "ln_x_w", "ln_x_b", "proj_a", "proj_b", "w_out", "norm_ffn2", "ffn2_gate", "ffn2_up",
        "ffn2_down", "norm_final")


def kernel(**inputs):
    import concourse.bacc as bacc
    from concourse.bass_utils import run_bass_kernel_spmd

    nc = bacc.Bacc("TRN2", target_bir_lowering=False, num_devices=1)
    arrays, args = {}, {}
    for name in _INS:
        a = np.ascontiguousarray(inputs[name])
        arrays[f"in_{name}"] = a
        args[name] = nc.dram_tensor(f"in_{name}", a.shape, mybir.dt.from_np(a.dtype), kind="ExternalInput").ap()
    arrays["in_consts"] = shape_constants()
    consts = nc.dram_tensor("in_consts", (P, C_ALL), F32, kind="ExternalInput").ap()
    out = nc.dram_tensor("out_x", (1, T, D), F32, kind="ExternalOutput").ap()
    trunk(nc, args, consts, out)
    r = run_bass_kernel_spmd(nc, [arrays], core_ids=[0])
    return r.results[0]["out_x"]
```

```python
from contextlib import ExitStack

import concourse.bass as bass
from concourse import mybir
import numpy as np

F32 = mybir.dt.float32
F32R = mybir.dt.float32r
ALU = mybir.AluOpType
ACT = mybir.ActivationFunctionType

P = 128
T = 256
D = 1024
KD = D // P
FF = 2816
FT = FF // P
W = 256
H = 8
HD = 64
WM = H * HD
HT = WM // P
C = 64
NCH = T // C
DL, AL, GL = 64, 64, 160
NB, MAXD = 32, 1024
RMS_EPS = 1e-6
GN_EPS = HD * 1e-5
NEG = -1e30
KS = (7, 7, 8)
NDOWN = len(KS) * D // W
EXP_HALF = float(np.exp(-0.5))

N_FFN1 = 0
N_DOWN1 = N_FFN1 + 2 * FF // W
N_RKV = N_DOWN1 + NDOWN
N_QK = N_RKV + 3 * WM // W
N_V = N_QK + 2 * WM // W
N_GATE = N_V + WM // W
N_PROJ = N_GATE + 2 * D // W
N_OUT = N_PROJ + D // W
N_FFN2 = N_OUT + D // W
N_DOWN2 = N_FFN2 + 2 * FF // W
N_ALL = N_DOWN2 + NDOWN

VECS = {}
for _name, _cols in (("norm_ffn1", KD), ("norm_mix", KD), ("norm_ffn2", KD), ("norm_final", KD),
                     ("mix_wag", 3 * KD), ("mix_rkv", 3 * HT), ("w0", HT), ("a0", HT), ("k_k", HT),
                     ("k_a", HT), ("r_k", HT), ("ln_x_w", HT), ("ln_x_b", HT)):
    VECS[_name] = (sum(c for _, c in VECS.values()), _cols)
NVEC = sum(c for _, c in VECS.values())

CONSTS = ("ident", "flip", "mean_d", "head_sum", "head_mean", "low_a", "low_r", "g2", "lev2", "lev4",
          "lev8", "lev16", "lev32")
CCOL = {name: i * P for i, name in enumerate(CONSTS)}
C_SUI, C_EPS = len(CONSTS) * P, len(CONSTS) * P + HD
C_HOT = C_EPS + 2
C_NEG = C_HOT + 384
C_ALL = C_NEG + 384


def shape_constants():
    c = np.zeros((P, C_ALL), np.float32)
    i = np.arange(P)[:, None]
    j = np.arange(P)[None, :]
    same = i // C == j // C
    eye = i == j
    mats = {
        "ident": eye, "flip": i + j == P - 1, "mean_d": np.full((P, P), 1.0 / D),
        "head_sum": i // HD == j // HD, "head_mean": (i // HD == j // HD) / HD,
        "low_a": same & (i < j), "low_r": same & (i <= j),
        "g2": eye | ((i // 2 == j // 2) & (i < j)),
    }
    for b in (2, 4, 8, 16, 32):
        mats[f"lev{b}"] = eye | ((i // (2 * b) == j // (2 * b)) & (i // b % 2 == 1) & (j // b % 2 == 0))
    for name, m in mats.items():
        c[:, CCOL[name]:CCOL[name] + P] = m
    c[:, C_SUI:C_SUI + HD] = i % HD == np.arange(HD)[None, :]
    c[:, C_EPS], c[:, C_EPS + 1] = RMS_EPS, GN_EPS
    dist = T - 1 - np.arange(384)
    n = np.maximum(dist, 0)
    exact = NB // 2
    large = exact + (np.log(np.maximum(n, exact).astype(np.float32) / np.float32(exact))
                     / np.float32(np.log(MAXD / exact)) * np.float32(NB - exact)).astype(np.int32)
    bucket = np.where(n < exact, n, np.minimum(large, NB - 1))
    c[:NB, C_HOT:C_HOT + 384] = np.arange(NB)[:, None] == bucket[None, :]
    c[:H, C_NEG:C_NEG + 384] = np.where(dist < 0, NEG, 0.0)[None, :]
    return c


SIGNALS = """
x_in0 x_in1 vec_in ident_in const_in gain1_in gain1_T gain1_ready vecT x_T x_loaded vec_ready
hi_ready lo_ready multiplied
sq_one sq_sum last_sq mean_sq rms_ready rstd_ready gained hhi_ready hlo_ready h_ready
gate_taken up_taken silu_done hid_prod hid_hi hid_lo down_first x_ffn_even x_ffn_odd
bias_row bias_row_sb bias_out bias_in bias_flip bias_ready
lora_in pads_zero h_diff xw_ready xa_ready xg_ready
mix_taken gate_sigmoid
tw_done ta_done tg_done tw_ready ta_ready tg_ready
z_done a_done g_done sig_w a_ready g_ready decay_ready 
dve_chain kk_sq_in kk_sq kk_ss kk_norm kk_inv kk_spread kk_scaled rkk_ready rkk_sum rk_wide rk_spread bonus_done
ab_ready kc_ready
s_done logits negmax exp_done prob_ready pt_done pt_ready pv_done ya_hi ya_lo
vt_done vt_ready tok_ready
pair_done pair_ready n_ready g2_ready t2_done
u_done iu_ready tt_done level_done t2_ready inv_ready invT_ready
x1_done as_done as_ready rh_done rh_ready phi_done phi_ready st_done st_ready
y_done y_ready gmean gdiff gsq gvar gstd gscale gspread yb_ready yb_hi yb_lo
proj_a pa_hi pa_lo merged m_hi m_lo x_mix
final_T final_copied final_copied_act out_stored
""".split()


def trunk(nc, A, consts, out):
    bias_dram = nc.dram_tensor("bias_rows", (H, 384), F32, kind="Internal").ap()
    with ExitStack() as ctx:
        def sb(name, shape, dt=F32, scope=ctx):
            return scope.enter_context(nc.sbuf_tensor(name, shape, dt))

        sg = {n: ctx.enter_context(nc.semaphore(n)) for n in SIGNALS}
        w_landed = [ctx.enter_context(nc.semaphore(f"w_landed{i}")) for i in range(2)]
        bank = [ctx.enter_context(nc.psum_tensor(f"bank{i}", [P, 512], F32)) for i in range(8)]

        raw = [sb(f"w_raw{i}", [P, KD, W]) for i in range(2)]
        whi = [sb(f"w_hi{i}", [P, KD, W], F32R) for i in range(2)]
        wlo = [sb(f"w_lo{i}", [P, KD, W], F32R) for i in range(2)]
        x = sb("x", [P, KD, T])
        cst = sb("cst", [P, C_ALL])
        vec = sb("vec", [P, NVEC])
        sq = sb("sq", [P, 2, T])
        sqsum = sb("sqsum", [P, 2, T])
        rstd = sb("rstd", [P, T + 2])
        bias_sb = sb("bias_sb", [H, 384])
        idle = sb("idle", [P, 2])

        def mat(name):
            return cst[:, CCOL[name]:CCOL[name] + P]

        ident, flip = mat("ident"), mat("flip")
        rstd2 = rstd[:, 0:T].unsqueeze(1).to_broadcast([P, 2, T])

        def v(name, i):
            return vec[:, VECS[name][0] + i:VECS[name][0] + i + 1]

        with ExitStack() as sc:
            h_f = sb("h_f", [P, KD, T], scope=sc)
            hhi_f = sb("hhi_f", [P, KD, T], F32R, scope=sc)
            hlo_f = sb("hlo_f", [P, KD, T], F32R, scope=sc)
            silu = sb("silu", [P, 2, T], scope=sc)
            prod = sb("prod", [P, 2, T], scope=sc)
            hid_hi = sb("hid_hi_t", [P, FT, T], F32R, scope=sc)
            hid_lo = sb("hid_lo_t", [P, FT, T], F32R, scope=sc)
            out_tok = sb("out_tok", [P, 2, D], scope=sc)
            x_tok = sb("x_tok", [P, 2, D], scope=sc)
            vec_rows = sb("vec_rows", [NVEC, P], scope=sc)
            rel = sb("rel", [NB, H], scope=sc)

        with ExitStack() as mix:
            def mb(name, shape, dt=F32, scope=mix):
                return sb(name, shape, dt, scope)

            r = mb("r", [P, HT, T])
            k = mb("k", [P, HT, T])
            vv = mb("v", [P, HT, T])
            dec = mb("dec", [P, HT * NCH, C + 1])
            one = mb("one", [P, HT * NCH, C + 1])
            run = mb("run", [P, HT * NCH, C + 1])
            kkn = mb("kkn", [P, HT, T])
            tmp = mb("tmp", [P, HT, T])
            aa = mb("aa", [P, HT, T])
            AR = mb("AR", [P, 2, HT, T])
            kt = mb("kt", [P, HT, T])
            gg = mb("gg", [P, HT, T])
            gates = mb("gates", [P, 2 * KD, T])
            yahi = mb("yahi", [P, HT, T], F32R)
            yalo = mb("yalo", [P, HT, T], F32R)
            ks = mb("ks", [P, 32])
            inv_run = dec[:, :, 1:C + 1]
            dpc = one[:, :, 0:C]
            bc, kc = kkn, tmp
            xa0, xa1 = gates[:, 0:KD], gates[:, KD:2 * KD]
            diff = AR[:, :, :, :].rearrange("p a j t -> p (a j) t")
            run_t = run[:, :, 1:C + 1]
            run_before = run[:, :, 0:C]
            run_end = run[:, :, C:C + 1]
            with ExitStack() as sc:
                h_m = mb("h_m", [P, KD, T + 1], scope=sc)
                rkv = mb("rkv", [P, 3 * HT, T + 1], scope=sc)
                tws = mb("tws", [DL, T], scope=sc)
                tas = mb("tas", [AL, T], scope=sc)
                tg0 = mb("tg0", [P, T], scope=sc)
                tg1 = mb("tg1", [GL - P, T], scope=sc)
                hhi_m = mb("hhi_m", [P, KD, T], F32R, scope=sc)
                hlo_m = mb("hlo_m", [P, KD, T], F32R, scope=sc)
                with ExitStack() as sc2:
                    laB = mb("laB", [AL, 2 * WM], scope=sc2)[:, 0:WM]
                    lgA = mb("lgA", [P, KD, GL], scope=sc2)
                flat = aa[:].rearrange("p j t -> p (j t)")
                lwA = flat[:, 0:KD * DL].rearrange("p (c n) -> p c n", c=KD)
                laA = flat[:, KD * DL:2 * KD * DL].rearrange("p (c n) -> p c n", c=KD)
                lwB = run[:].rearrange("p a b -> p (a b)")[0:DL, 0:WM]
                flat = gg[:].rearrange("p j t -> p (j t)")
                lgB0, lgB1 = flat[:, 0:WM], flat[0:GL - P, WM:2 * WM]
                qk = mb("qk", [P, 2 * HT, T], scope=sc)
                va = mb("va", [P, 2, WM], scope=sc)
                idec = mb("idec", [P, HT * NCH, C + 1], scope=sc)
            with ExitStack() as sc:
                bias_w = mb("bias_w", [P, H, T], scope=sc)
                bias = mb("bias", [P, H, T], scope=sc)
                lg = mb("lg", [P, 2, 3 * P], scope=sc)
                pt = mb("pt", [P, 2, 3 * P], scope=sc)
                stat = mb("stat", [P, H, 8], scope=sc)
            with ExitStack() as sc:
                vt = mb("vt", [P, 2, WM], scope=sc)
                bct = mb("bct", [P, 2, WM], scope=sc)
                kct = mb("kct", [P, 2, WM], scope=sc)
                NR = mb("NR", [P, H, 2, P], scope=sc)
                KK = mb("KK", [P, H, 2, P], scope=sc)
                G = mb("G", [P, H, P], scope=sc)
                TT = mb("TT", [P, H, P], scope=sc)
                IU = mb("IU", [P, H, P], scope=sc)
                phi = mb("phi", [P, 2, 2, HT, C], scope=sc)
                state = mb("state", [P, NCH, HT, C], scope=sc)
                AX = mb("AX", [P, 2, H, P], scope=sc)
                gs = mb("gs", [P, 2 * H], scope=sc)
                gx = mb("gx", [P, HT, P], scope=sc)
                AS = IU
            with ExitStack() as sc:
                ybhi = mb("ybhi", [P, HT, T], F32R, scope=sc)
                yblo = mb("yblo", [P, HT, T], F32R, scope=sc)
                pa = mb("pa", [P, 2, 2, T], scope=sc)
                mg = mb("mg", [P, KD, T], scope=sc)
                mhi = mb("mhi", [P, KD, T], F32R, scope=sc)
                mlo = mb("mlo", [P, KD, T], F32R, scope=sc)

        h_m1 = h_m[:, :, 1:T + 1]
        NORM_BANKS = ((0, 1), (4, 5))
        FINAL = ((0, 1), (5, 6))
        yy = r
        gate_w = [A["ffn1_gate"][0].rearrange("(c p) f -> p c f", p=P),
                  A["ffn2_gate"][0].rearrange("(c p) f -> p c f", p=P)]
        up_w = [A["ffn1_up"][0].rearrange("(c p) f -> p c f", p=P),
                A["ffn2_up"][0].rearrange("(c p) f -> p c f", p=P)]
        down_w = [A["ffn1_down"][0].rearrange("(c p) f -> p c f", p=P),
                  A["ffn2_down"][0].rearrange("(c p) f -> p c f", p=P)]
        w_in = A["w_in"][0].rearrange("(c p) f -> p c f", p=P)
        proj_w = [A["proj_a"][0].rearrange("(c p) f -> p c f", p=P),
                  A["proj_b"][0].rearrange("(c p) f -> p c f", p=P)]
        w_out = A["w_out"][0].rearrange("(c p) f -> p c f", p=P)
        FFN = ((0, N_FFN1, N_DOWN1), (1, N_FFN2, N_DOWN2))
        NG = FF // W

        def vector_rows(engine, name, signal):
            (at, cols), src = VECS[name], A[name]
            flat = {1: "d -> d", 2: "l d -> (l d)", 3: "l a d -> (l a d)"}[len(src.shape)]
            src = (src if len(src.shape) == 1 else src.rearrange(flat)).rearrange("(c p) -> c p", p=P)
            engine.dma_start(vec_rows[at:at + cols, :], src).then_inc(signal, 16)

        block = ctx.enter_context(nc.Block())

        @block.sync
        def _(sp):
            def load(n, half, slot, src, kts=KD, first=0):
                if not isinstance(n, int) or n >= 2:
                    sp.wait_ge(sg["lo_ready"], n - 1)
                sp.dma_start(raw[slot][:, first:first + kts], src).then_inc(w_landed[slot], 16)

            xs = A["x"][0].rearrange("(j p) d -> p j d", p=P)
            sp.dma_start(cst[:, 0:P], consts[:, 0:P]).then_inc(sg["ident_in"], 16)
            for half in range(2):
                ds = slice(half * D // 2, (half + 1) * D // 2)
                sp.dma_start(x_tok[:, :, ds], xs[:, :, ds]).then_inc(sg[f"x_in{half}"], 16)

            for f, base, down in FFN:
                load(base, base // 2, 0, gate_w[f][:, :, 0:W])
                if f == 0:
                    sp.dma_start(cst[:, P:C_ALL], consts[:, P:C_ALL]).then_inc(sg["const_in"], 16)
                load(base + 1, base // 2, 1, up_w[f][:, :, 0:W])
                if f == 0:
                    for name in list(VECS)[1:]:
                        vector_rows(sp, name, sg["vec_in"])
                    sp.dma_start(rel[:], A["rel_bias"]).then_inc(sg["vec_in"], 16)
                with sp.Fori(1, NG) as i:
                    load(2 * i + base, None, 0, gate_w[f][:, :, bass.ts(i, W)])
                    load(2 * i + base + 1, None, 1, up_w[f][:, :, bass.ts(i, W)])
                with sp.Fori(0, D // W // 2) as jp:
                    for t in range(6):
                        k0 = sum(KS[:t % 3])
                        load(6 * jp + (down + t), None, t % 2,
                             down_w[f][:, k0:k0 + KS[t % 3], bass.ds(jp * (2 * W) + (t // 3) * W, W)], KS[t % 3])
                if f == 0:
                    with sp.Fori(0, 3 * WM // W // 2) as i:
                        for s in range(2):
                            load(2 * i + N_RKV + s, None, s,
                                 w_in[:, :, bass.ds(i * (2 * W) + (3 * WM + s * W), W)])
                    with sp.Fori(0, 3 * WM // W // 2) as i:
                        for s in range(2):
                            load(2 * i + N_QK + s, None, s, w_in[:, :, bass.ds(i * (2 * W) + s * W, W)])
                    with sp.Fori(0, 2 * D // W // 2) as i:
                        for s in range(2):
                            load(2 * i + N_GATE + s, None, s,
                                 w_in[:, :, bass.ds(i * (2 * W) + (6 * WM + s * W), W)])
                    with sp.Fori(0, D // W // 2) as i:
                        for s in range(2):
                            cols = bass.ds(i * (2 * W) + s * W, W)
                            sp.wait_ge(sg["lo_ready"], 2 * i + N_PROJ + s - 1)
                            sp.dma_start(raw[s][:, 0:HT], proj_w[0][:, :, cols]).then_inc(w_landed[s], 16)
                            sp.dma_start(raw[s][:, HT:2 * HT], proj_w[1][:, :, cols]).then_inc(w_landed[s], 16)
                    with sp.Fori(0, D // W // 2) as i:
                        for s in range(2):
                            load(2 * i + N_OUT + s, None, s, w_out[:, :, bass.ds(i * (2 * W) + s * W, W)])
            os = out[0].rearrange("(j p) d -> p j d", p=P)
            for g in range(2):
                for j in range(2):
                    sp.wait_ge((sg["final_copied"], sg["final_copied_act"])[j], g + 1)
                    ds = slice(g * D // 2, (g + 1) * D // 2)
                    sp.dma_start(os[:, j, ds], out_tok[:, j, ds]).then_inc(sg["out_stored"], 16)
            sp.wait_ge(sg["out_stored"], 4 * 16)

        def landings(n):
            return n // 2 + 1 + max(0, min(n // 2, N_OUT // 2 - 1) - N_PROJ // 2 + 1)

        EXTRA2 = landings(N_FFN2) - (N_FFN2 // 2 + 1)

        @block.gpsimd
        def _(pool):
            def squares(q, signal, first, step, pairs=4):
                for c in range(pairs):
                    pool.wait_ge(signal, first + c * step)
                    pair = x[:, 2 * c:2 * c + 2]
                    if c == 0:
                        if q:
                            pool.wait_ge(sg["mean_sq"], q)
                        nc.gpsimd.tensor_tensor(sqsum[:], pair, pair, ALU.mult).then_inc(sg["sq_sum"], 1)
                    else:
                        pool.wait_ge(sg["sq_sum"], 4 * q + c)
                        nc.gpsimd.tensor_tensor(sq[:], pair, pair, ALU.mult).then_inc(sg["sq_one"], 1)
                        pool.wait_ge(sg["sq_one"], 3 * q + c)
                        nc.gpsimd.tensor_tensor(sqsum[:], sqsum[:], sq[:], ALU.add).then_inc(sg["sq_sum"], 1)

            squares(0, sg["x_loaded"], 1, 1)
            pool.wait_ge(sg["bias_row_sb"], 1)
            pool.dma_start(bias_dram, bias_sb[:]).then_inc(sg["bias_out"], 16)
            pool.wait_ge(sg["bias_out"], 16)
            squares(1, sg["x_ffn_odd"], 2, 1)
            pool.wait_ge(sg["x_ffn_odd"], 1 + KD // 2)
            nc.gpsimd.memset(one[:], 0.0).then_inc(sg["pads_zero"], 1)
            nc.gpsimd.memset(dec[:, :, 0:1], 0.0).then_inc(sg["pads_zero"], 1)
            nc.gpsimd.memset(idec[:, :, 0:1], 0.0).then_inc(sg["pads_zero"], 1)
            nc.gpsimd.memset(rkv[:, :, 0:1], 0.0).then_inc(sg["pads_zero"], 1)
            pool.wait_ge(sg["pads_zero"], 4)
            nc.gpsimd.memset(one[:, :, 0:1], 1.0).then_inc(sg["pads_zero"], 1)
            for t, name in ((lwA, "w_lora_a"), (laA, "a_lora_a"), (lgA[:], "g_lora_a")):
                pool.dma_start(t, A[name][0].rearrange("(c p) n -> p c n", p=P)).then_inc(sg["lora_in"], 16)
            for t, name in ((lwB, "w_lora_b"), (laB, "a_lora_b")):
                pool.dma_start(t, A[name][0]).then_inc(sg["lora_in"], 16)
            pool.dma_start(lgB0, A["g_lora_b"][0][0:P]).then_inc(sg["lora_in"], 16)
            pool.dma_start(lgB1, A["g_lora_b"][0][P:GL]).then_inc(sg["lora_in"], 16)
            pool.wait_ge(sg["h_ready"], 1)
            nc.gpsimd.tensor_tensor(diff, h_m[:, :, 0:T], h_m[:, :, 1:T + 1], ALU.subtract).then_inc(sg["h_diff"], 1)
            pool.wait_ge(sg["h_diff"], 1)

            def mixed(which, dst, signal):
                for c in range(KD):
                    nc.gpsimd.tensor_scalar(dst[:, c], diff[:, c], v("mix_wag", which * KD + c), None,
                                            ALU.mult).then_inc(signal, 1)
                pool.wait_ge(signal, KD)
                nc.gpsimd.tensor_tensor(dst, dst, h_m[:, :, 1:T + 1], ALU.add).then_inc(signal, 1)

            mixed(0, xa0, sg["xw_ready"])
            pool.wait_ge(sg["tw_done"], 1)
            mixed(2, xa0, sg["xg_ready"])

            pool.wait_ge(sg["xa_ready"], KD)
            pool.wait_ge(sg["xg_ready"], KD + 1)
            pool.dma_start(bias_w[:], bass.AP(bias_dram.tensor, 0, [[1, P], [384, H], [1, T]])).then_inc(sg["bias_in"], 16)
            squares(2, sg["x_mix"], 1, 1)
            squares(3, sg["x_ffn_odd"], 2 + KD // 2, 1, 3)

        @block.scalar
        def _(act):
            def hi(n, half, slot, kts=KD):
                act.wait_ge(w_landed[slot], 16 * half)
                if not isinstance(n, int) or n >= 2:
                    act.wait_ge(sg["multiplied"], n - 1)
                nc.scalar.activation(whi[slot][:, 0:kts], raw[slot][:, 0:kts], ACT.Copy).then_inc(sg["hi_ready"], 1)

            def hi_at(n, kts=KD):
                hi(n, landings(n), n % 2, kts)

            def rms_root(q, cols=slice(0, T + 2)):
                act.wait_ge(sg["mean_sq"], q + 1)
                nc.scalar.activation(rstd[:, cols], bank[4][:, cols], ACT.Sqrt,
                                     bias=cst[:, C_EPS:C_EPS + 1]).then_inc(sg["rms_ready"], 1)

            def h_hi(q, j, src, dst):
                act.wait_ge(sg["gained"], q * KD + 2 * j + 2)
                nc.scalar.activation(dst[:, 2 * j:2 * j + 2], src[:, 2 * j:2 * j + 2],
                                     ACT.Copy).then_inc(sg["hhi_ready"], 1)

            def ffn(f, base, down):
                extra = EXTRA2 if f else 0
                g0 = NG * f

                def body(i, nexts):
                    nexts[0]()
                    act.wait_ge(sg["gate_taken"], i + (g0 + 1))
                    nc.scalar.activation(silu[:], silu[:], ACT.Silu).then_inc(sg["silu_done"], 1)
                    nexts[1]()
                    act.wait_ge(sg["hid_prod"], i + (g0 + 1))
                    nc.scalar.activation(hid_hi[:, bass.ds(i * 2, 2)], prod[:], ACT.Copy).then_inc(sg["hid_hi"], 1)

                def nexts(i):
                    return [lambda s=s: hi(2 * i + (base + 2 + s), i + (base // 2 + 2 + extra), s) for s in range(2)]

                body(0, nexts(0))
                with act.Fori(1, NG - 1) as i:
                    body(i, nexts(i))
                body(NG - 1, [lambda s=s: hi(down + s, down // 2 + 1 + extra, s) for s in range(2)])

                for s in range(NDOWN):
                    if s == NDOWN - 1 and f == 0:
                        h_hi(1, 3, h_m1, hhi_m)
                    if s + 2 < NDOWN:
                        hi(down + s + 2, (down + s + 2) // 2 + 1 + extra, s % 2, KS[(s + 2) % 3])
                    elif f == 0:
                        hi(down + s + 2, (down + s + 2) // 2 + 1, s % 2)
                    if s % 3 == 2 and s < NDOWN - 1 and f == 0:
                        h_hi(1, s // 3, h_m1, hhi_m)

            vector_rows(act, "norm_ffn1", sg["gain1_in"])
            hi_at(0)
            for j in range(4):
                h_hi(0, j, h_f, hhi_f)
            hi_at(1)
            rms_root(0)
            act.wait_ge(sg["vecT"], 1)
            nc.scalar.activation(vec[:, KD:NVEC], bank[5][:, KD:NVEC], ACT.Copy).then_inc(sg["vec_ready"], 1)
            ffn(0, N_FFN1, N_DOWN1)

            def attend(i):
                if 1 <= i <= H:
                    act.wait_ge(sg["pt_done"], i)
                    if i >= 3:
                        act.wait_ge(sg["pv_done"], i - 2)
                    nc.scalar.activation(pt[:, (i - 1) % 2], bank[2 + (i - 1) % 2][:, 0:3 * P],
                                         ACT.Copy).then_inc(sg["pt_ready"], 1)
                if i < H:
                    act.wait_ge(sg["negmax"], i + 1)
                    for q, (lo_, hi_) in enumerate(((0, 2 * P), (2 * P, 3 * P))):
                        nc.scalar.activation(lg[:, i % 2, lo_:hi_], lg[:, i % 2, lo_:hi_], ACT.Exp,
                                             bias=stat[:, i, 2 + q:3 + q],
                                             accum_out=stat[:, i, 4 + q:5 + q]).then_inc(sg["exp_done"], 1)
                if i >= 2 and i % 2 == 1:
                    act.wait_ge(sg["pv_done"], i - 1)
                    j = (i - 3) // 2
                    nc.scalar.activation(yahi[:, j], bank[4 + j % 2][:, 0:T], ACT.Copy).then_inc(sg["ya_hi"], 1)

            n = N_RKV
            rms_root(1)
            for c in range(6):
                hi_at(n + c + 2)
            act.wait_ge(sg["tw_done"], 1)
            nc.scalar.activation(tws[:], bank[2][0:DL, 0:T], ACT.Tanh).then_inc(sg["tw_ready"], 1)
            act.wait_ge(sg["ta_done"], 1)
            nc.scalar.activation(tas[:], bank[3][0:AL, 0:T], ACT.Copy).then_inc(sg["ta_ready"], 1)
            act.wait_ge(sg["z_done"], 1)
            for j in range(HT):
                nc.scalar.activation(tmp[:, j], bank[6 + j // 2][:, (j % 2) * T:(j % 2 + 1) * T], ACT.Sigmoid,
                                     bias=v("w0", j)).then_inc(sg["sig_w"], 1)
            act.wait_ge(sg["a_done"], 1)
            for j in range(HT):
                nc.scalar.activation(aa[:, j], bank[2 + j // 2][:, (j % 2) * T:(j % 2 + 1) * T], ACT.Sigmoid,
                                     bias=v("a0", j)).then_inc(sg["a_ready"], 1)
            act.wait_ge(sg["sig_w"], HT)
            nc.scalar.activation(dec[:, :, 1:C + 1], tmp[:].rearrange("p j (q c) -> p (j q) c", c=C), ACT.Exp,
                                 scale=-EXP_HALF).then_inc(sg["decay_ready"], 1)
            act.wait_ge(sg["pads_zero"], 5)
            nc.scalar.activation(idec[:, :, 1:C + 1], tmp[:].rearrange("p j (q c) -> p (j q) c", c=C), ACT.Exp,
                                 scale=EXP_HALF).then_inc(sg["decay_ready"], 1)
            for c in range(6, 20):
                n = N_RKV + c
                if c < 19:
                    hi_at(n + 2)
                if c == 7:
                    act.wait_ge(sg["kk_sq_in"], 1)
                    act.wait_ge(sg["decay_ready"], 2)
                    nc.scalar.activation(tmp[:], kkn[:], ACT.Square).then_inc(sg["kk_sq"], 1)
                if c == 8:
                    act.wait_ge(sg["tg_done"], 1)
                    nc.scalar.activation(tg0[:], bank[4][:, 0:T], ACT.Sigmoid).then_inc(sg["tg_ready"], 1)
                    nc.scalar.activation(tg1[:], bank[5][0:GL - P, 0:T], ACT.Sigmoid).then_inc(sg["tg_ready"], 1)
                    act.wait_ge(sg["kk_ss"], 1)
                    nc.scalar.activation(ks[:, 0:16], bank[2][:, 0:16], ACT.Sqrt).then_inc(sg["kk_norm"], 1)
                if c == 9:
                    act.wait_ge(sg["g_done"], 1)
                    for j in range(2):
                        nc.scalar.activation(gg[:, 2 * j:2 * j + 2],
                                             bank[4 + j][:].rearrange("p (m t) -> p m t", m=2),
                                             ACT.Copy).then_inc(sg["g_ready"], 1)
                if c in (10, 11):
                    act.wait_ge(sg["bias_flip"], c - 9)
                    for q in range(2 * (c - 10), 2 * (c - 10) + 2):
                        nc.scalar.activation(bias[:, 2 * q:2 * q + 2],
                                             bank[4 + q % 2][:].rearrange("p (h t) -> p h t", h=2),
                                             ACT.Copy).then_inc(sg["bias_ready"], 1)
                if c >= 11:
                    attend(c - 11)

            for q in range(4):
                if q == 1:
                    attend(9)
                act.wait_ge(sg["vt_done"], 2 * q + 1)
                arr = (vt, None, bct, kct)[q]
                dst = AX[:, 0, :, 0:HD] if arr is None else arr[:, 0].rearrange("p (h n) -> p h n", n=HD)
                nc.scalar.activation(dst, bank[0][:].rearrange("p (h n) -> p h n", n=HD),
                                     ACT.Copy).then_inc(sg["vt_ready"], 1)
            def norm_square(J):
                ts = slice(J * P, (J + 1) * P)
                act.wait_ge(sg["gdiff"], J + 1)
                nc.scalar.activation(tmp[:, :, ts], yy[:, :, ts], ACT.Square).then_inc(sg["gsq"], 1)

            def norm_root(J):
                act.wait_ge(sg["gvar"], J + 1)
                nc.scalar.activation(gs[:, 0:H], bank[NORM_BANKS[J][1]][:, 0:H], ACT.Sqrt,
                                     bias=cst[:, C_EPS + 1:C_EPS + 2]).then_inc(sg["gstd"], 1)

            for J in range(2):
                for g in range(2):
                    hs = slice(4 * g, 4 * g + 4)
                    act.wait_ge(sg["t2_done"], 2 * J + g + 1)
                    nc.scalar.activation(TT[:, hs], bank[6 + g][:].rearrange("p (h n) -> p h n", n=P),
                                         ACT.Copy).then_inc(sg["t2_ready"], 1)
                if J:
                    norm_square(0)
                for lev in range(5):
                    if J and lev == 2:
                        norm_root(0)
                    for g in range(2):
                        hs = slice(4 * g, 4 * g + 4)
                        act.wait_ge(sg["level_done"], J * 10 + lev * 2 + g + 1)
                        nc.scalar.activation(G[:, hs], bank[6 + g][:].rearrange("p (h n) -> p h n", n=P),
                                             ACT.Copy).then_inc(sg["invT_ready"], 1)
                for g in range(2):
                    act.wait_ge(sg["as_done"], 2 * J + g + 1)
                    nc.scalar.activation(AS[:, 4 * g:4 * g + 4], bank[2 + g][:].rearrange("p (h n) -> p h n", n=P),
                                         ACT.Copy).then_inc(sg["as_ready"], 1)
                if J == 0:
                    hi_at(N_PROJ + 1)
                    act.wait_ge(sg["mix_taken"], 20)
                    for i in range(8):
                        gate = gates[:, 2 * i:2 * i + 2]
                        nc.scalar.activation(gate, gate, ACT.Sigmoid).then_inc(sg["gate_sigmoid"], 1)
                act.wait_ge(sg["y_done"], J + 1)
                for b in range(2):
                    nc.scalar.activation(yy[64 * b:64 * b + 64, :, J * P:(J + 1) * P],
                                         bank[b][64 * b:64 * b + 64, :].rearrange("p (j t) -> p j t", t=P),
                                         ACT.Copy).then_inc(sg["y_ready"], 1)
            for J in range(2):
                if J:
                    norm_square(1)
                    norm_root(1)
                act.wait_ge(sg["yb_ready"], J + 1)
                nc.scalar.activation(ybhi[:, :, J * P:(J + 1) * P], kt[:, :, J * P:(J + 1) * P],
                                     ACT.Copy).then_inc(sg["yb_hi"], 1)
            def hi_half(c, half):
                if half == 0:
                    act.wait_ge(w_landed[c % 2], 16 * landings(N_PROJ + c))
                    act.wait_ge(sg["proj_a"], c - 1)
                else:
                    act.wait_ge(sg["multiplied"], N_PROJ + c - 1)
                ks_ = slice(half * HT, (half + 1) * HT)
                nc.scalar.activation(whi[c % 2][:, ks_], raw[c % 2][:, ks_],
                                     ACT.Copy).then_inc(sg["hi_ready"] if half else sg["pa_hi"], 1)

            hi_half(2, 0)
            hi_half(3, 0)
            for c in range(4):
                if c < 2:
                    hi_half(c + 2, 1)
                if c == 2:
                    hi_at(N_PROJ + c + 2)
                act.wait_ge(sg["merged"], c + 1)
                nc.scalar.activation(mhi[:, 2 * c:2 * c + 2], mg[:, 2 * c:2 * c + 2], ACT.Copy).then_inc(sg["m_hi"], 1)
                if c == 3:
                    hi_at(N_PROJ + c + 2)
            for c in range(4):
                if c == 3:
                    h_hi(2, c, h_f, hhi_f)
                hi_at(N_OUT + c + 2)
                if c < 3:
                    h_hi(2, c, h_f, hhi_f)
            rms_root(2)
            ffn(1, N_FFN2, N_DOWN2)
            act.wait_ge(sg["x_ffn_odd"], 1 + KD)
            nc.scalar.activation(prod[:], x[:, KD - 2:KD], ACT.Square).then_inc(sg["last_sq"], 1)
            rms_root(3, slice(T, T + 2))
            act.wait_ge(sg["rstd_ready"], 4)
            act.wait_ge(sg["final_T"], 2)
            for g in range(2):
                nc.scalar.activation(out_tok[:, 1, g * 512:(g + 1) * 512], bank[FINAL[g][1]][:], ACT.Identity,
                                     scale=rstd[:, T + 1:T + 2]).then_inc(sg["final_copied_act"], 1)

        @block.vector
        def _(dve):
            chain = [0]

            def link(ins):
                chain[0] += 1
                ins.then_inc(sg["dve_chain"], 1)
                dve.wait_ge(sg["dve_chain"], chain[0])

            def lo(n, slot, kts=KD):
                dve.wait_ge(sg["hi_ready"], n + 1)
                nc.vector.tensor_tensor(wlo[slot][:, 0:kts], raw[slot][:, 0:kts],
                                        whi[slot][:, 0:kts].bitcast(F32), ALU.subtract).then_inc(sg["lo_ready"], 1)

            GAINS = ("norm_ffn1", "norm_mix", "norm_ffn2", "norm_final")

            def gain(q, j, dst):
                for m in range(2):
                    nc.vector.tensor_scalar(dst[:, 2 * j + m], x[:, 2 * j + m], v(GAINS[q], 2 * j + m), None,
                                            ALU.mult).then_inc(sg["gained"], 1)

            def h_lo(q, j, src, hh, hl):
                dve.wait_ge(sg["hhi_ready"], 4 * q + j + 1)
                nc.vector.tensor_tensor(hl[:, 2 * j:2 * j + 2], src[:, 2 * j:2 * j + 2],
                                        hh[:, 2 * j:2 * j + 2].bitcast(F32), ALU.subtract).then_inc(sg["hlo_ready"], 1)

            def inverse_rms(q, cols=slice(0, T + 2)):
                dve.wait_ge(sg["rms_ready"], q + 1)
                nc.vector.reciprocal(rstd[:, cols], rstd[:, cols]).then_inc(sg["rstd_ready"], 1)
                dve.wait_ge(sg["rstd_ready"], q + 1)

            def ffn(f, base, down):
                g0 = NG * f

                def body(i, nexts):
                    dve.wait_ge(sg["multiplied"], i * 2 + (base + 1))
                    if not isinstance(i, int) or i + g0 > 0:
                        dve.wait_ge(sg["hid_prod"], i + g0)
                    nc.vector.tensor_tensor(silu[:], bank[0][:].rearrange("p (m t) -> p m t", m=2), rstd2,
                                            ALU.mult).then_inc(sg["gate_taken"], 1)
                    nexts[0]()
                    dve.wait_ge(sg["multiplied"], i * 2 + (base + 2))
                    if not isinstance(i, int) or i + g0 > 0:
                        dve.wait_ge(sg["hid_lo"], i + g0)
                    nc.vector.tensor_tensor(prod[:], bank[1][:].rearrange("p (m t) -> p m t", m=2), rstd2,
                                            ALU.mult).then_inc(sg["up_taken"], 1)
                    dve.wait_ge(sg["up_taken"], i + (g0 + 1))
                    dve.wait_ge(sg["silu_done"], i + (g0 + 1))
                    nc.vector.tensor_tensor(prod[:], silu[:], prod[:], ALU.mult).then_inc(sg["hid_prod"], 1)
                    nexts[1]()
                    dve.wait_ge(sg["hid_hi"], i + (g0 + 1))
                    nc.vector.tensor_tensor(hid_lo[:, bass.ds(i * 2, 2)], prod[:],
                                            hid_hi[:, bass.ds(i * 2, 2)].bitcast(F32),
                                            ALU.subtract).then_inc(sg["hid_lo"], 1)

                def nexts(i):
                    return [lambda s=s: lo(2 * i + (base + 2 + s), s) for s in range(2)]

                body(0, nexts(0))
                with dve.Fori(1, NG - 1) as i:
                    body(i, nexts(i))
                body(NG - 1, [lambda s=s: lo(down + s, s) for s in range(2)])

                q, hv = 2 * f + 1, (h_m1, h_f)[f]
                for s in range(NDOWN):
                    j = s // 3
                    if s == NDOWN - 1 and f == 0:
                        h_lo(q, j, hv, hhi_m, hlo_m)
                    if s + 2 < NDOWN or f == 0:
                        lo(down + s + 2, s % 2, KS[(s + 2) % 3] if s + 2 < NDOWN else KD)
                    if s % 3 == 1:
                        for m in range(2):
                            if m == 0:
                                dve.wait_ge(sg["down_first"], j + f * (D // W) + 1)
                            else:
                                dve.wait_ge(sg["multiplied"], down + 3 * j + 3)
                            nc.vector.scalar_tensor_tensor(out=x[:, 2 * j + m], in0=bank[2 + m][:, 0:T], scalar=0.5,
                                                           in1=x[:, 2 * j + m], op0=ALU.mult, op1=ALU.add)\
                                .then_inc((sg["x_ffn_even"], sg["x_ffn_odd"])[m], 1)
                        for signal in ("x_ffn_even", "x_ffn_odd"):
                            dve.wait_ge(sg[signal], j + f * (D // W) + 2)
                        gain(q, j, hv)
                    if s % 3 == 2 and s < NDOWN - 1 and f == 0:
                        h_lo(q, j, hv, hhi_m, hlo_m)

            nc.vector.memset(idle[:, 0:1], 0.0).then_inc(sg["x_ffn_even"], 1)
            nc.vector.memset(idle[:, 1:2], 0.0).then_inc(sg["x_ffn_odd"], 1)
            for q in range(4):
                dve.wait_ge(sg["x_T"], q + 1)
                nc.vector.tensor_copy(x[:, 2 * q:2 * q + 2], bank[q][:].rearrange("p (c t) -> p c t", c=2))\
                    .then_inc(sg["x_loaded"], 1)
            dve.wait_ge(sg["gain1_T"], 1)
            nc.vector.tensor_copy(vec[:, 0:KD], bank[7][:, 0:KD]).then_inc(sg["gain1_ready"], 1)
            dve.wait_ge(sg["gain1_ready"], 1)
            dve.wait_ge(sg["x_loaded"], 4)
            for j in range(4):
                gain(0, j, h_f)
            lo(0, 0)
            for j in range(4):
                h_lo(0, j, h_f, hhi_f, hlo_f)
            lo(1, 1)
            inverse_rms(0)
            dve.wait_ge(sg["bias_row"], 1)
            nc.vector.tensor_tensor(bias_sb[:], bank[6][0:H, 0:384], cst[0:H, C_NEG:C_NEG + 384],
                                    ALU.add).then_inc(sg["bias_row_sb"], 1)
            dve.wait_ge(sg["vec_ready"], 1)
            ffn(0, N_FFN1, N_DOWN1)
            link(nc.vector.memset(h_m[:, :, 0:1], 0.0))
            inverse_rms(1)
            dve.wait_ge(sg["hlo_ready"], 8)
            nc.vector.tensor_tensor(h_m1, h_m1, rstd[:, 0:T].unsqueeze(1).to_broadcast([P, KD, T]),
                                    ALU.mult).then_inc(sg["h_ready"], 1)

            def take(c):
                dve.wait_ge(sg["multiplied"], N_RKV + c + 1)
                src = bank[c % 2][:].rearrange("p (m t) -> p m t", m=2)
                if c in (10, 11):
                    for j in range(2):
                        last = nc.vector.tensor_scalar(va[:, j, (c - 10) * W:(c - 9) * W], src[:, j],
                                                       rstd[:, T + j:T + j + 1], None, ALU.mult)
                elif c in (6, 7):
                    last = nc.vector.scalar_tensor_tensor(out=qk[:, 2 * (c - 6):2 * (c - 6) + 2], in0=src,
                                                          scalar=HD ** -0.5, in1=rstd2, op0=ALU.mult, op1=ALU.mult)
                else:
                    dst = (rkv[:, 2 * c:2 * c + 2, 1:T + 1] if c < 6 else qk[:, 2 * (c - 6):2 * (c - 6) + 2] if c < 10
                           else gates[:, 2 * (c - 12):2 * (c - 12) + 2])
                    last = nc.vector.tensor_tensor(dst, src, rstd2, ALU.mult)
                last.then_inc(sg["mix_taken"], 1)

            def shift_mix(which, dst, chunk):
                dve.wait_ge(sg["mix_taken"], chunk)
                src = rkv[:, which * HT:(which + 1) * HT]
                link(nc.vector.tensor_tensor(kt[:], src[:, :, 0:T], src[:, :, 1:T + 1], ALU.subtract))
                for j in range(HT):
                    last = nc.vector.scalar_tensor_tensor(out=dst[:, j], in0=kt[:, j], scalar=v("mix_rkv", which * HT + j),
                                                          in1=src[:, j, 1:T + 1], op0=ALU.mult, op1=ALU.add)
                link(last)

            view = lambda t: t[:].rearrange("p j (q c) -> p (j q) c", c=C)
            wide = lambda t: t[:].rearrange("p j (q c) -> p (j q) c", c=HD)
            bank2 = lambda i: bank[i][:].rearrange("p (m t) -> p m t", m=2)
            def logits(i):
                dve.wait_ge(sg["bias_ready"], i // 2 + 1)
                dve.wait_ge(sg["s_done"], i + 1)
                if i >= 2:
                    dve.wait_ge(sg["pt_done"], i - 1)
                s = bank[6 + i % 2]
                nc.vector.tensor_tensor(lg[:, i % 2, 0:2 * P], s[:, 0:2 * P], bias[:, i, 0:2 * P],
                                        ALU.add).then_inc(sg["logits"], 1)
                nc.vector.tensor_tensor(lg[:, i % 2, 2 * P:3 * P], s[:, 2 * P:3 * P], bias[:, i, P:2 * P],
                                        ALU.add).then_inc(sg["logits"], 1)
                dve.wait_ge(sg["logits"], 2 * i + 1)
                nc.vector.reduce_max(stat[:, i, 0:1], lg[:, i % 2, 0:2 * P], mybir.AxisListType.X)
                dve.wait_ge(sg["logits"], 2 * i + 2)
                link(nc.vector.reduce_max(stat[:, i, 1:2], lg[:, i % 2, 2 * P:3 * P], mybir.AxisListType.X))
                nc.vector.tensor_scalar(stat[:, i, 2:4], stat[:, i, 0:2], -1.0, None,
                                        ALU.mult).then_inc(sg["negmax"], 1)

            def probabilities(i):
                if i < H:
                    dve.wait_ge(sg["exp_done"], 2 * i + 2)
                    link(nc.vector.reciprocal(stat[:, i, 6:8], stat[:, i, 4:6]))
                    nc.vector.tensor_scalar(lg[:, i % 2, 0:2 * P], lg[:, i % 2, 0:2 * P], stat[:, i, 6:7], None,
                                            ALU.mult).then_inc(sg["prob_ready"], 1)
                    nc.vector.tensor_scalar(lg[:, i % 2, 2 * P:3 * P], lg[:, i % 2, 2 * P:3 * P], stat[:, i, 7:8],
                                            None, ALU.mult).then_inc(sg["prob_ready"], 1)
                if i >= 4 and i % 2 == 0:
                    j = (i - 4) // 2
                    dve.wait_ge(sg["ya_hi"], j + 1)
                    nc.vector.tensor_tensor(yalo[:, j], bank[4 + j % 2][:, 0:T], yahi[:, j].bitcast(F32),
                                            ALU.subtract).then_inc(sg["ya_lo"], 1)

            for c in range(20):
                take(c)
                if 11 <= c < 11 + H:
                    logits(c - 11)
                if c < 19:
                    lo(N_RKV + c + 2, c % 2)
                if c == 2:
                    dve.wait_ge(sg["h_diff"], 1)
                    for i in range(KD):
                        nc.vector.scalar_tensor_tensor(out=xa1[:, i], in0=diff[:, i], scalar=v("mix_wag", KD + i),
                                                       in1=h_m1[:, i], op0=ALU.mult,
                                                       op1=ALU.add).then_inc(sg["xa_ready"], 1)
                if c == 1:
                    dve.wait_ge(sg["pads_zero"], 5)
                    shift_mix(0, r, 2)
                if c == 3:
                    shift_mix(1, k, 4)
                    for j in range(HT):
                        last = nc.vector.tensor_scalar(kkn[:, j], k[:, j], v("k_k", j), None, ALU.mult)
                    last.then_inc(sg["kk_sq_in"], 1)
                if c == 5:
                    shift_mix(2, vv, 6)
                if c == 6:
                    dve.wait_ge(sg["decay_ready"], 2)
                    dve.wait_ge(sg["pads_zero"], 5)
                    link(nc.vector.tensor_tensor_scan(run[:].rearrange("p a b -> p (a b)"),
                                                      dec[:].rearrange("p a b -> p (a b)"),
                                                      one[:].rearrange("p a b -> p (a b)"), 0.0,
                                                      ALU.mult, ALU.add))
                    link(nc.vector.tensor_tensor_scan(dec[:].rearrange("p a b -> p (a b)"),
                                                      idec[:].rearrange("p a b -> p (a b)"),
                                                      one[:].rearrange("p a b -> p (a b)"), 0.0,
                                                      ALU.mult, ALU.add))
                    dve.wait_ge(sg["a_ready"], HT)
                    for j in range(HT):
                        last = nc.vector.tensor_scalar(kt[:, j], aa[:, j], 1.0, v("k_a", j), ALU.subtract, ALU.mult)
                    link(last)
                    link(nc.vector.scalar_tensor_tensor(out=k[:], in0=kt[:], scalar=1.0, in1=k[:],
                                                        op0=ALU.add, op1=ALU.mult))
                if c == 7:
                    nc.vector.tensor_tensor(view(kt), view(k), inv_run, ALU.mult)
                    dve.wait_ge(sg["xg_ready"], KD + 1)
                    link(nc.vector.tensor_tensor(AR[:, 1].rearrange("p j (q c) -> p (j q) c", c=C), view(r), run_t,
                                                 ALU.mult))
                    nc.vector.tensor_tensor(dpc, cst[:, C_SUI:C_SUI + C].unsqueeze(1).to_broadcast([P, HT * NCH, C]),
                                            run_end.to_broadcast([P, HT * NCH, C]), ALU.mult).then_inc(sg["ab_ready"], 1)
                if c == 8:
                    for j in range(HT):
                        last = nc.vector.scalar_tensor_tensor(out=r[:, j], in0=r[:, j], scalar=v("r_k", j), in1=k[:, j],
                                                              op0=ALU.mult, op1=ALU.mult)
                    last.then_inc(sg["rkk_ready"], 1)
                if c == 9:
                    dve.wait_ge(sg["kk_norm"], 1)
                    link(nc.vector.tensor_scalar(ks[:, 0:16], ks[:, 0:16], 1e-12, None, ALU.max))
                    link(nc.vector.reciprocal(ks[:, 16:32], ks[:, 0:16]))
                    nc.vector.tensor_copy(wide(tmp), ks[:, 16:32].unsqueeze(2).to_broadcast([P, 16, HD]))\
                        .then_inc(sg["kk_inv"], 1)
                    dve.wait_ge(sg["rkk_sum"], 1)
                    nc.vector.tensor_copy(wide(r), bank[6][:, 0:16].unsqueeze(2).to_broadcast([P, 16, HD]))\
                        .then_inc(sg["rk_wide"], 1)
                if c == 10:
                    dve.wait_ge(sg["kk_spread"], 1)
                    for j in range(2):
                        nc.vector.tensor_tensor(kkn[:, 2 * j:2 * j + 2], kkn[:, 2 * j:2 * j + 2], bank2(2 + j),
                                                ALU.mult).then_inc(sg["kk_scaled"], 1)
                    dve.wait_ge(sg["rk_spread"], 1)
                    for j in range(2):
                        nc.vector.tensor_tensor(k[:, 2 * j:2 * j + 2], vv[:, 2 * j:2 * j + 2], bank2(6 + j),
                                                ALU.mult).then_inc(sg["bonus_done"], 1)
                if c == 11:
                    dve.wait_ge(sg["kk_scaled"], 2)
                    link(nc.vector.tensor_tensor(aa[:], kkn[:], aa[:], ALU.mult))
                if c == 12:
                    link(nc.vector.tensor_tensor(view(aa), view(aa), inv_run, ALU.mult))
                    nc.vector.scalar_tensor_tensor(out=AR[:, 0].rearrange("p j (q c) -> p (j q) c", c=C),
                                                   in0=view(kkn), scalar=-1.0, in1=run_before,
                                                   op0=ALU.mult, op1=ALU.mult).then_inc(sg["ab_ready"], 1)
                if c == 13:
                    dve.wait_ge(sg["ab_ready"], 2)
                    nc.vector.tensor_tensor(view(bc), view(aa), run_end.to_broadcast([P, HT * NCH, C]),
                                            ALU.mult).then_inc(sg["kc_ready"], 1)
                    nc.vector.tensor_tensor(view(kc), view(kt), run_end.to_broadcast([P, HT * NCH, C]),
                                            ALU.mult).then_inc(sg["kc_ready"], 1)
                if c == 15:
                    dve.wait_ge(sg["bonus_done"], 2)
                    for j in range(HT):
                        last = nc.vector.tensor_scalar(k[:, j], k[:, j], v("ln_x_b", j), None, ALU.add)
                    last.then_inc(sg["bonus_done"], 1)
                if c >= 11:
                    probabilities(c - 11)
            for q in range(4):
                if q == 1:
                    dve.wait_ge(sg["ya_hi"], 4)
                    nc.vector.tensor_tensor(yalo[:, 3], bank[5][:, 0:T], yahi[:, 3].bitcast(F32),
                                            ALU.subtract).then_inc(sg["ya_lo"], 1)
                dve.wait_ge(sg["vt_done"], 2 * q + 2)
                arr = (vt, None, bct, kct)[q]
                dst = AX[:, 1, :, 0:HD] if arr is None else arr[:, 1].rearrange("p (h n) -> p h n", n=HD)
                nc.vector.tensor_copy(dst, bank[1][:].rearrange("p (h n) -> p h n", n=HD)).then_inc(sg["tok_ready"], 1)
            eye4 = ident.unsqueeze(1).to_broadcast([P, 4, P])

            def norm_centre(J):
                ts = slice(J * P, (J + 1) * P)
                dve.wait_ge(sg["gmean"], J + 1)
                nc.vector.tensor_tensor(yy[:, :, ts], yy[:, :, ts],
                                        bank[NORM_BANKS[J][0]][:].rearrange("p (j t) -> p j t", j=HT),
                                        ALU.subtract).then_inc(sg["gdiff"], 1)

            def norm_scale(J):
                dve.wait_ge(sg["gstd"], J + 1)
                link(nc.vector.reciprocal(gs[:, H:2 * H], gs[:, 0:H]))
                nc.vector.tensor_copy(gx[:].rearrange("p j (a n) -> p (j a) n", a=2),
                                      gs[:, H:2 * H].unsqueeze(2).to_broadcast([P, H, HD])).then_inc(sg["gscale"], 1)

            def norm_apply(J):
                ts = slice(J * P, (J + 1) * P)
                dve.wait_ge(sg["gspread"], J + 1)
                link(nc.vector.tensor_tensor(yy[:, :, ts], yy[:, :, ts],
                                             bank[NORM_BANKS[J][0]][:].rearrange("p (j t) -> p j t", j=HT), ALU.mult))
                dve.wait_ge(sg["bonus_done"], 3)
                for j in range(HT):
                    last = nc.vector.scalar_tensor_tensor(out=yy[:, j, ts], in0=yy[:, j, ts], scalar=v("ln_x_w", j),
                                                          in1=k[:, j, ts], op0=ALU.mult, op1=ALU.add)
                link(last)
                dve.wait_ge(sg["g_ready"], 2)
                nc.vector.tensor_tensor(kt[:, :, ts], yy[:, :, ts], gg[:, :, ts], ALU.mult).then_inc(sg["yb_ready"], 1)

            for J in range(2):
                def mask(name, n):
                    return mat(name).unsqueeze(1).to_broadcast([P, n, P])

                for q in range(8):
                    dve.wait_ge(sg["pair_done"], 8 * J + q + 1)
                    par, pos, dst = q % 2, q // 2 % 2, (NR, KK)[q // 4]
                    heads = dst[:, 4 * pos + par:4 * pos + par + 3:2]
                    src = bank[2 + q % 4][:].rearrange("p (h a t) -> p h a t", h=2, a=2)
                    nc.vector.tensor_tensor(heads[:, :, 0], src[:, :, 0], mask("low_a", 2), ALU.mult)
                    nc.vector.tensor_tensor(heads[:, :, 1], src[:, :, 1], mask("low_r", 2),
                                            ALU.mult).then_inc(sg["pair_ready"], 1)
                    if q == 3:
                        dve.wait_ge(sg["pair_ready"], 8 * J + 4)
                        for g in range(2):
                            hs = slice(4 * g, 4 * g + 4)
                            nc.vector.tensor_tensor(NR[:, hs, 0], NR[:, hs, 0], eye4, ALU.add).then_inc(sg["n_ready"], 1)
                        for g in range(2):
                            hs = slice(4 * g, 4 * g + 4)
                            dve.wait_ge(sg["n_ready"], 2 * J + g + 1)
                            nc.vector.tensor_tensor(G[:, hs], NR[:, hs, 0], mask("g2", 4), ALU.mult).then_inc(sg["g2_ready"], 1)
                if J:
                    norm_centre(0)
                for lev in range(5):
                    if J and lev == 3:
                        norm_scale(0)
                    for g in range(2):
                        hs = slice(4 * g, 4 * g + 4)
                        dve.wait_ge(sg["u_done"], J * 10 + lev * 2 + g + 1)
                        nc.vector.tensor_tensor(IU[:, hs], bank[4 + g][:].rearrange("p (h n) -> p h n", n=P),
                                                mask(f"lev{2 << lev}", 4), ALU.mult).then_inc(sg["iu_ready"], 1)
                    if lev < 4:
                        for g in range(2):
                            hs = slice(4 * g, 4 * g + 4)
                            dve.wait_ge(sg["tt_done"], J * 8 + lev * 2 + g + 1)
                            nc.vector.tensor_copy(TT[:, hs], bank[2 + g][:].rearrange("p (h n) -> p h n", n=P))\
                                .then_inc(sg["inv_ready"], 1)
                dve.wait_ge(sg["x1_done"], J + 1)
                nc.vector.tensor_copy(AX[:, J, :, HD:P], bank[2][:].rearrange("p (h n) -> p h n", n=HD))\
                    .then_inc(sg["tok_ready"], 1)
                if J:
                    norm_apply(0)
                dve.wait_ge(sg["rh_done"], J + 1)
                rs = AR[:, 1, :, J * P:(J + 1) * P]
                nc.vector.tensor_tensor(rs, bank[5][:].rearrange("p (j t) -> p j t", t=P), rs, ALU.add)\
                    .then_inc(sg["rh_ready"], 1)
                if J == 0:
                    lo(N_PROJ + 1, 1)
                dve.wait_ge(sg["phi_done"], J + 1)
                for c in range(2):
                    src = bank[6 + c][:].rearrange("p (a j n) -> p a j n", a=2, j=HT)
                    ends = dpc.rearrange("p (j q) n -> p j q n", q=NCH)[:, :, 2 * J + c]
                    nc.vector.tensor_tensor(phi[:, c, 0], src[:, 0], ends, ALU.add)
                    last = nc.vector.tensor_copy(phi[:, c, 1], src[:, 1])
                    if J == 0 and c == 0:
                        nc.vector.tensor_copy(state[:, 1], src[:, 1])
                last.then_inc(sg["phi_ready"], 1)
                dve.wait_ge(sg["phi_ready"], J + 1)
                for c in range(2):
                    q = 2 * J + c
                    if 1 <= q <= 2:
                        dve.wait_ge(sg["st_done"], q)
                        for b in range(2):
                            bs = slice(64 * b, 64 * b + 64)
                            nc.vector.tensor_tensor(state[bs, q + 1], phi[bs, c, 1],
                                                    bank[2 + b][bs, 0:HT * C].rearrange("p (j n) -> p j n", n=C),
                                                    ALU.add).then_inc(sg["st_ready"], 1)
            norm_centre(1)
            norm_scale(1)
            for J in range(2):
                if J:
                    norm_apply(1)
                dve.wait_ge(sg["yb_hi"], J + 1)
                ts = slice(J * P, (J + 1) * P)
                nc.vector.tensor_tensor(yblo[:, :, ts], kt[:, :, ts], ybhi[:, :, ts].bitcast(F32),
                                        ALU.subtract).then_inc(sg["yb_lo"], 1)
            dve.wait_ge(sg["gate_sigmoid"], 8)

            def gated_a(c):
                dve.wait_ge(sg["proj_a"], c + 1)
                link(nc.vector.tensor_tensor(pa[:, c % 2], gates[:, 2 * c:2 * c + 2], bank2(2 * (c % 2)), ALU.mult))

            def lo_half(c, half):
                if half == 0:
                    dve.wait_ge(sg["pa_hi"], c - 1)
                else:
                    dve.wait_ge(sg["hi_ready"], N_PROJ + c + 1)
                ks_ = slice(half * HT, (half + 1) * HT)
                nc.vector.tensor_tensor(wlo[c % 2][:, ks_], raw[c % 2][:, ks_], whi[c % 2][:, ks_].bitcast(F32),
                                        ALU.subtract).then_inc(sg["lo_ready"] if half else sg["pa_lo"], 1)

            gated_a(0)
            gated_a(1)
            lo_half(2, 0)
            lo_half(3, 0)
            for c in range(4):
                if c >= 2:
                    gated_a(c)
                dve.wait_ge(sg["multiplied"], N_PROJ + c + 1)
                link(nc.vector.tensor_tensor(mg[:, 2 * c:2 * c + 2], gates[:, KD + 2 * c:KD + 2 * c + 2],
                                             bank2(2 * (c % 2) + 1), ALU.mult))
                nc.vector.tensor_tensor(mg[:, 2 * c:2 * c + 2], mg[:, 2 * c:2 * c + 2], pa[:, c % 2],
                                        ALU.add).then_inc(sg["merged"], 1)
                if c < 2:
                    lo_half(c + 2, 1)
                if c == 2:
                    lo(N_PROJ + c + 2, c % 2)
                dve.wait_ge(sg["m_hi"], c + 1)
                nc.vector.tensor_tensor(mlo[:, 2 * c:2 * c + 2], mg[:, 2 * c:2 * c + 2],
                                        mhi[:, 2 * c:2 * c + 2].bitcast(F32), ALU.subtract).then_inc(sg["m_lo"], 1)
                if c == 3:
                    lo(N_PROJ + c + 2, c % 2)
            for c in range(4):
                dve.wait_ge(sg["multiplied"], N_OUT + c + 1)
                nc.vector.tensor_tensor(x[:, 2 * c:2 * c + 2], x[:, 2 * c:2 * c + 2], bank2(4 + c % 2),
                                        ALU.add).then_inc(sg["x_mix"], 1)
                dve.wait_ge(sg["x_mix"], c + 1)
                gain(2, c, h_f)
                if c == 3:
                    h_lo(2, c, h_f, hhi_f, hlo_f)
                lo(N_OUT + c + 2, c % 2)
                if c < 3:
                    h_lo(2, c, h_f, hhi_f, hlo_f)
            inverse_rms(2)
            ffn(1, N_FFN2, N_DOWN2)
            inverse_rms(3, slice(T, T + 2))
            dve.wait_ge(sg["final_T"], 2)
            for g in range(2):
                nc.vector.tensor_scalar(out_tok[:, 0, g * 512:(g + 1) * 512], bank[FINAL[g][0]][:],
                                        rstd[:, T:T + 1], None, ALU.mult).then_inc(sg["final_copied"], 1)

        @block.tensor
        def _(pe):
            mm = nc.tensor.matmul

            def part(dst, lhsT, rhs, start=False):
                return mm(dst, lhsT, rhs, start=start, stop=True, skip_group_check=True)

            def three(dst, slot, k_, cols, xh, xl, start, stop):
                mm(dst, whi[slot][:, k_, cols], xl, start=start, stop=False)
                mm(dst, wlo[slot][:, k_, cols], xh, start=False, stop=False)
                return mm(dst, whi[slot][:, k_, cols], xh, start=False, stop=stop)

            def mean_square(q, cols=True):
                pe.wait_ge(sg["sq_sum"], 4 * q + (4 if cols else 3))
                if cols:
                    for a in range(2):
                        part(bank[4][:, 0:T], mat("mean_d"), sqsum[:, a], a == 0)
                sums = [sqsum[:, 0], sqsum[:, 1]]
                if not cols:
                    pe.wait_ge(sg["last_sq"], 1)
                    sums += [prod[:, 0], prod[:, 1]]
                for j in range(2):
                    for a, total in enumerate(sums):
                        last = part(bank[4][:, T + j:T + j + 1], total[:, j * P:(j + 1) * P],
                                    mat("mean_d")[:, 0:1], not cols and a + j == 0)
                last.then_inc(sg["mean_sq"], 1)

            def columns(dst, slot, hh, hl, q=None, ks=range(KD)):
                for m in range(2):
                    if q is not None and m == 1:
                        mean_square(q)
                    for c in ks:
                        if q is not None and m == 0 and c % 2 == 0:
                            pe.wait_ge(sg["hlo_ready"], 4 * q + c // 2 + 1)
                        last = three(dst[:, m * T:(m + 1) * T], slot, c, slice(m * P, (m + 1) * P),
                                     hh[:, c], hl[:, c], c == ks[0], c == ks[-1])
                return last

            def ffn(f, base, down, q):
                g0 = NG * f

                def chunk(i, s, q_=None):
                    pe.wait_ge(sg["lo_ready"], 2 * i + (base + 1 + s))
                    if not isinstance(i, int) or i + g0 > 0:
                        pe.wait_ge((sg["gate_taken"], sg["up_taken"])[s], i + g0)
                    columns(bank[s], s, hhi_f, hlo_f, q_).then_inc(sg["multiplied"], 1)

                chunk(0, 0, q)
                if f == 0:
                    pe.wait_ge(sg["vec_in"], 16 * len(VECS))
                    nc.tensor.transpose(bank[5][:, 0:NVEC], vec_rows[:], ident[0:NVEC, 0:NVEC]).then_inc(sg["vecT"], 1)
                    mm(bank[6][0:H, 0:384], rel[:], cst[0:NB, C_HOT:C_HOT + 384], start=True, stop=True)\
                        .then_inc(sg["bias_row"], 1)
                chunk(0, 1)
                with pe.Fori(1, NG) as i:
                    chunk(i, 0)
                    chunk(i, 1)

                with pe.Fori(0, D // W // 2) as jp:
                    for t in range(6):
                        part_, s, half = t % 3, t % 2, t // 3
                        k0 = sum(KS[:part_])
                        pe.wait_ge(sg["lo_ready"], 6 * jp + (down + t + 1))
                        pe.wait_ge(sg["hid_lo"], g0 + (k0 + KS[part_] + 1) // 2)
                        for m in range(2):
                            if part_ == 0:
                                pe.wait_ge((sg["x_ffn_even"], sg["x_ffn_odd"])[m], 2 * jp + (f * (D // W) + half + 1))
                            for c in range(KS[part_]):
                                last = three(bank[2 + m][:, 0:T], s, c, slice(m * P, (m + 1) * P),
                                             hid_hi[:, k0 + c], hid_lo[:, k0 + c],
                                             k0 + c == 0, k0 + c == FT - 1)
                            if part_ == 2 and m == 0:
                                last.then_inc(sg["down_first"], 1)
                        last.then_inc(sg["multiplied"], 1)

            pe.wait_ge(sg["ident_in"], 16)
            for q in range(4):
                pe.wait_ge(sg[f"x_in{q // 2}"], 16)
                for c in range(2):
                    for j in range(2):
                        last = nc.tensor.transpose(bank[q][:, c * T + j * P:c * T + (j + 1) * P],
                                                   x_tok[:, j, (2 * q + c) * P:(2 * q + c + 1) * P], ident)
                last.then_inc(sg["x_T"], 1)
            pe.wait_ge(sg["gain1_in"], 16)
            nc.tensor.transpose(bank[7][:, 0:KD], vec_rows[0:KD], ident[0:KD, 0:KD]).then_inc(sg["gain1_T"], 1)
            pe.wait_ge(sg["const_in"], 16)
            pe.wait_ge(sg["x_loaded"], 4)
            ffn(0, N_FFN1, N_DOWN1, 0)

            def product(c, s, q=None):
                pe.wait_ge(sg["lo_ready"], N_RKV + c + 1)
                if not isinstance(c, int) or c >= 2:
                    pe.wait_ge(sg["mix_taken"], c - 1)
                columns(bank[s], s, hhi_m, hlo_m, q).then_inc(sg["multiplied"], 1)

            product(0, 0, 1)
            product(1, 1)
            with pe.Fori(2, 6, 2) as c:
                product(c, 0)
                product(c + 1, 1)

            def lora_in(dst, w, xs, rows):
                for c in range(KD):
                    last = mm(dst, w[:, c, rows], xs[:, c], start=c == 0, stop=c == KD - 1)
                return last

            pe.wait_ge(sg["lora_in"], 16 * 7)
            pe.wait_ge(sg["xw_ready"], KD + 1)
            lora_in(bank[2][0:DL, 0:T], lwA, xa0, slice(0, DL)).then_inc(sg["tw_done"], 1)
            pe.wait_ge(sg["xa_ready"], KD)
            lora_in(bank[3][0:AL, 0:T], laA, xa1, slice(0, AL)).then_inc(sg["ta_done"], 1)
            pe.wait_ge(sg["tw_ready"], 1)
            for j in range(HT):
                last = part(bank[6 + j // 2][:, (j % 2) * T:(j % 2 + 1) * T], lwB[:, j * P:(j + 1) * P], tws[:],
                            True)
            last.then_inc(sg["z_done"], 1)
            pe.wait_ge(sg["ta_ready"], 1)
            for j in range(HT):
                last = part(bank[2 + j // 2][:, (j % 2) * T:(j % 2 + 1) * T], laB[:, j * P:(j + 1) * P], tas[:],
                            True)
            last.then_inc(sg["a_done"], 1)
            product(6, 0)
            product(7, 1)
            pe.wait_ge(sg["xg_ready"], KD + 1)
            lora_in(bank[4][:, 0:T], lgA, xa0, slice(0, P))
            lora_in(bank[5][0:GL - P, 0:T], lgA, xa0, slice(P, GL)).then_inc(sg["tg_done"], 1)
            def head_sums(dst, src):
                for J in range(2):
                    for j in range(HT):
                        last = part(dst[:, J * H + 2 * j:J * H + 2 * j + 2], src[:, j, J * P:(J + 1) * P],
                                    mat("head_sum")[:, 0:P:HD], J + j == 0)
                return last

            def spread(b, src):
                flat = src[:].rearrange("p j t -> p (j t)")
                for J in range(2):
                    for j in range(HT):
                        last = nc.tensor.transpose(bank[b + j // 2][:, (j % 2) * T + J * P:(j % 2) * T + (J + 1) * P],
                                                   flat[:, J * WM + j * P:J * WM + (j + 1) * P], ident)
                return last

            product(8, 0)
            pe.wait_ge(sg["kk_sq"], 1)
            pe.wait_ge(sg["a_ready"], HT)
            head_sums(bank[2], tmp).then_inc(sg["kk_ss"], 1)
            product(9, 1)
            pe.wait_ge(sg["rkk_ready"], 1)
            head_sums(bank[6], r).then_inc(sg["rkk_sum"], 1)
            pe.wait_ge(sg["tg_ready"], 2)
            for j in range(HT):
                dst = bank[4 + j // 2][:, (j % 2) * T:(j % 2 + 1) * T]
                mm(dst, lgB0[:, j * P:(j + 1) * P], tg0[:], start=True, stop=False)
                last = mm(dst, lgB1[:, j * P:(j + 1) * P], tg1[:], start=False, stop=True)
            last.then_inc(sg["g_done"], 1)
            pe.wait_ge(sg["kk_inv"], 1)
            spread(2, tmp).then_inc(sg["kk_spread"], 1)

            def attend(i):
                if i < H:
                    j, bs = i // 2, slice(64 * (i % 2), 64 * (i % 2) + 64)
                    if i == 0:
                        pe.wait_ge(sg["bonus_done"], 2)
                        pe.wait_ge(sg["mix_taken"], 10)
                    if i >= 2:
                        pe.wait_ge(sg["logits"], 2 * (i - 1))
                    part(bank[6 + i % 2][:, 0:2 * P], qk[bs, j, P:2 * P], qk[bs, HT + j], True)
                    part(bank[6 + i % 2][:, 2 * P:3 * P], qk[bs, j, 0:P], qk[bs, HT + j, 0:P])\
                        .then_inc(sg["s_done"], 1)
                if 1 <= i <= H:
                    h = i - 1
                    pe.wait_ge(sg["prob_ready"], 2 * (h + 1))
                    if h >= 2:
                        pe.wait_ge(sg["pt_ready"], h - 1)
                    b = bank[2 + h % 2]
                    nc.tensor.transpose(b[:, 0:P], lg[:, h % 2, 2 * P:3 * P], ident)
                    nc.tensor.transpose(b[:, P:2 * P], lg[:, h % 2, 0:P], ident)
                    nc.tensor.transpose(b[:, 2 * P:3 * P], lg[:, h % 2, P:2 * P], ident).then_inc(sg["pt_done"], 1)
                if i >= 2:
                    h = i - 2
                    j, bs = h // 2, slice(64 * (h % 2), 64 * (h % 2) + 64)
                    if h == 0:
                        pe.wait_ge(sg["mix_taken"], 12)
                        pe.wait_ge(sg["bias_ready"], 4)
                    pe.wait_ge(sg["pt_ready"], h + 1)
                    if j >= 2:
                        pe.wait_ge(sg["ya_lo"], j - 1)
                    part(bank[4 + j % 2][bs, 0:T], va[:, 0, h * HD:(h + 1) * HD], pt[:, h % 2, 0:T], True)
                    part(bank[4 + j % 2][bs, P:T], va[:, 1, h * HD:(h + 1) * HD], pt[:, h % 2, T:3 * P])\
                        .then_inc(sg["pv_done"], 1)

            for c in range(10, 12):
                pe.wait_ge(sg["lo_ready"], N_RKV + c + 1)
                pe.wait_ge(sg["mix_taken"], c - 1)
                for j in range(2):
                    ts = slice(j * P, (j + 1) * P)
                    dst = bank[c % 2][:, j * T:(j + 1) * T]
                    for k_ in range(KD):
                        mm(dst, hlo_m[:, k_, ts], whi[c % 2][:, k_], start=k_ == 0, stop=False)
                        mm(dst, hhi_m[:, k_, ts], wlo[c % 2][:, k_], start=False, stop=False)
                        last = mm(dst, hhi_m[:, k_, ts], whi[c % 2][:, k_], start=False, stop=k_ == KD - 1)
                last.then_inc(sg["multiplied"], 1)
                if c == 10:
                    pe.wait_ge(sg["rk_wide"], 1)
                    spread(6, r).then_inc(sg["rk_spread"], 1)
                pe.wait_ge(sg["bias_in"], 16)
                if c == 10:
                    pe.wait_ge(sg["g_ready"], 2)
                else:
                    pe.wait_ge(sg["bias_ready"], 2)
                for q in range(2 * (c - 10), 2 * (c - 10) + 2):
                    last = mm(bank[4 + q % 2][:], flip, bias_w[:, 2 * q:2 * q + 2], start=True, stop=True)
                last.then_inc(sg["bias_flip"], 1)
            attend(0)
            for c in range(12, 20):
                product(c, c % 2)
                attend(c - 11)

            pe.wait_ge(sg["kc_ready"], 2)
            for q in range(4):
                if q == 1:
                    attend(9)
                for J in range(2):
                    if q:
                        pe.wait_ge((sg["vt_ready"], sg["tok_ready"])[J], q)
                    else:
                        pe.wait_ge(sg["mix_taken"], 20)
                    for j in range(HT):
                        src = (vv[:, j], AR[:, 0, j], bc[:, j], kc[:, j])[q]
                        last = nc.tensor.transpose(bank[J][:, j * P:(j + 1) * P], src[:, J * P:(J + 1) * P], ident)
                    last.then_inc(sg["vt_done"], 1)
            def norm_mean(J):
                pe.wait_ge(sg["y_ready"], 2 * J + 2)
                mm(bank[NORM_BANKS[J][0]][:], mat("head_mean"), yy[:, :, J * P:(J + 1) * P], start=True,
                   stop=True).then_inc(sg["gmean"], 1)

            def norm_var(J):
                pe.wait_ge(sg["gsq"], J + 1)
                for j in range(HT):
                    last = part(bank[NORM_BANKS[J][1]][:, 2 * j:2 * j + 2], tmp[:, j, J * P:(J + 1) * P],
                                mat("head_mean")[:, 0:P:HD], j == 0)
                last.then_inc(sg["gvar"], 1)

            def norm_spread(J):
                pe.wait_ge(sg["gscale"], J + 1)
                for j in range(HT):
                    last = nc.tensor.transpose(bank[NORM_BANKS[J][0]][:, j * P:(j + 1) * P], gx[:, j], ident)
                last.then_inc(sg["gspread"], 1)

            pe.wait_ge(sg["ya_lo"], HT)
            for J in range(2):
                sl = slice(J * P, (J + 1) * P)
                pe.wait_ge(sg["ab_ready"], 2)
                if J:
                    pe.wait_ge(sg["st_ready"], 2)
                for q in range(8):
                    par, pos = q % 2, q // 2 % 2
                    bs = slice(64 * par, 64 * par + 64)
                    if q >= 4:
                        pe.wait_ge(sg["pair_ready"], 8 * J + q - 3)
                    for t in range(2):
                        j = 2 * pos + t
                        last = part(bank[2 + q % 4][:, t * 2 * P:(t + 1) * 2 * P], (aa, kt)[q // 4][bs, j, sl],
                                    AR[bs, :, j, sl], t == 0)
                    last.then_inc(sg["pair_done"], 1)
                for g in range(2):
                    pe.wait_ge(sg["g2_ready"], 2 * J + g + 1)
                    for i in range(4):
                        last = nc.tensor.transpose(bank[6 + g][:, i * P:(i + 1) * P], G[:, 4 * g + i], ident)
                    last.then_inc(sg["t2_done"], 1)
                if J:
                    norm_mean(0)
                for lev in range(5):
                    for g in range(2):
                        if lev == 0:
                            pe.wait_ge(sg["t2_ready"], 2 * J + g + 1)
                            pe.wait_ge(sg["pair_ready"], 8 * J + 7 + g)
                        else:
                            pe.wait_ge(sg["inv_ready"], 8 * J + 2 * (lev - 1) + g + 1)
                            for i in range(4):
                                last = nc.tensor.transpose(bank[6 + g][:, i * P:(i + 1) * P], TT[:, 4 * g + i], ident)
                            last.then_inc(sg["level_done"], 1)
                        for i in range(4):
                            last = part(bank[4 + g][:, i * P:(i + 1) * P], NR[:, 4 * g + i, 0], TT[:, 4 * g + i],
                                        i == 0)
                        last.then_inc(sg["u_done"], 1)
                    if lev == 4:
                        for h in range(H):
                            last = part(bank[2][:, h * HD:(h + 1) * HD], KK[:, h, 0], vt[:, J, h * HD:(h + 1) * HD], h == 0)
                        last.then_inc(sg["x1_done"], 1)
                    for g in range(2):
                        pe.wait_ge(sg["iu_ready"], 10 * J + 2 * lev + g + 1)
                        if lev:
                            pe.wait_ge(sg["invT_ready"], 10 * J + 2 * (lev - 1) + g + 1)
                        for i in range(4):
                            h = 4 * g + i
                            if lev < 4:
                                last = part(bank[2 + g][:, i * P:(i + 1) * P], G[:, h], IU[:, h], i == 0)
                            else:
                                last = part(bank[6 + g][:, i * P:(i + 1) * P], IU[:, h], G[:, h], i == 0)
                        last.then_inc(sg["tt_done"] if lev < 4 else sg["level_done"], 1)
                    if J and lev == 0:
                        norm_var(0)
                    if J and lev == 3:
                        norm_spread(0)
                pe.wait_ge(sg["tok_ready"], 5 + J)
                for g in range(2):
                    pe.wait_ge(sg["invT_ready"], 10 * J + 8 + g + 1)
                    for i in range(4):
                        last = part(bank[2 + g][:, i * P:(i + 1) * P], G[:, 4 * g + i], AX[:, J, 4 * g + i], i == 0)
                    last.then_inc(sg["as_done"], 1)
                for h in range(H):
                    if h % 4 == 0:
                        pe.wait_ge(sg["as_ready"], 2 * J + h // 4 + 1)
                    j, bs = h // 2, slice(64 * (h % 2), 64 * (h % 2) + 64)
                    last = part(bank[5][bs, j * P:(j + 1) * P], AS[:, h, 0:HD], NR[:, h, 1], j == 0)
                last.then_inc(sg["rh_done"], 1)
                for h in range(H):
                    j, bs, hc = h // 2, slice(64 * (h % 2), 64 * (h % 2) + 64), slice(h * HD, (h + 1) * HD)
                    for c in range(2):
                        cs = slice(64 * c, 64 * c + 64)
                        part(bank[6 + c][bs, j * C:(j + 1) * C], AS[cs, h, 0:HD], bct[cs, J, hc], j == 0)
                for h in range(H):
                    j, bs, hc = h // 2, slice(64 * (h % 2), 64 * (h % 2) + 64), slice(h * HD, (h + 1) * HD)
                    for c in range(2):
                        cs = slice(64 * c, 64 * c + 64)
                        psi = bank[6 + c][bs, (HT + j) * C:(HT + j + 1) * C]
                        part(psi, bct[cs, J, hc], AS[cs, h, HD:P])
                        last = part(psi, kct[cs, J, hc], vt[cs, J, hc])
                last.then_inc(sg["phi_done"], 1)
                if J:
                    pe.wait_ge(sg["yb_ready"], 1)
                for h in range(H):
                    j, bs, hc = h // 2, slice(64 * (h % 2), 64 * (h % 2) + 64), slice(h * HD, (h + 1) * HD)
                    dst = bank[h % 2][bs, j * P:(j + 1) * P]
                    part(dst, AS[:, h, HD:P], NR[:, h, 1], j == 0)
                    part(dst, vt[:, J, hc], KK[:, h, 1])
                pe.wait_ge(sg["phi_ready"], J + 1)
                pe.wait_ge(sg["rh_ready"], J + 1)
                for c in range(2):
                    q = 2 * J + c
                    if q == 0:
                        continue
                    if q >= 2:
                        pe.wait_ge(sg["st_ready"], 2 * (q - 1))
                    if q < NCH - 1:
                        for h in range(H):
                            j, bs = h // 2, slice(64 * (h % 2), 64 * (h % 2) + 64)
                            last = part(bank[2 + h % 2][bs, j * C:(j + 1) * C], phi[bs, c, 0, j], state[bs, q, j],
                                        j == 0)
                        last.then_inc(sg["st_done"], 1)
                    for h in range(H):
                        j, bs = h // 2, slice(64 * (h % 2), 64 * (h % 2) + 64)
                        last = part(bank[h % 2][bs, j * P + c * C:j * P + (c + 1) * C], state[bs, q, j],
                                    AR[bs, 1, j, q * C:(q + 1) * C])
                last.then_inc(sg["y_done"], 1)
            def proj_a(c, m):
                if m == 0 and c < 2:
                    pe.wait_ge(sg["lo_ready"], N_PROJ + c + 1)
                if m == 0 and c >= 2:
                    pe.wait_ge(sg["pa_lo"], c - 1)
                    pe.wait_ge(sg["merged"], c - 1)
                s = c % 2
                for j in range(HT):
                    last = three(bank[2 * s][:, m * T:(m + 1) * T], s, j, slice(m * P, (m + 1) * P),
                                 yahi[:, j], yalo[:, j], j == 0, j == HT - 1)
                if m == 1:
                    last.then_inc(sg["proj_a"], 1)

            norm_mean(1)
            proj_a(0, 0)
            norm_var(1)
            proj_a(0, 1)
            norm_spread(1)
            proj_a(1, 0)
            proj_a(1, 1)
            pe.wait_ge(sg["yb_lo"], 2)
            for c in range(4):
                s = c % 2
                if c >= 2:
                    proj_a(c, 0)
                    proj_a(c, 1)
                    pe.wait_ge(sg["lo_ready"], N_PROJ + c + 1)
                for m in range(2):
                    for j in range(HT):
                        last = three(bank[2 * s + 1][:, m * T:(m + 1) * T], s, HT + j, slice(m * P, (m + 1) * P),
                                     ybhi[:, j], yblo[:, j], j == 0, j == HT - 1)
                last.then_inc(sg["multiplied"], 1)
            for c in range(4):
                pe.wait_ge(sg["lo_ready"], N_OUT + c + 1)
                if c >= 2:
                    pe.wait_ge(sg["x_mix"], c - 1)
                for m in range(2):
                    for k_ in range(KD):
                        if c == 0 and m == 0 and k_ % 2 == 0:
                            pe.wait_ge(sg["m_lo"], k_ // 2 + 1)
                        last = three(bank[4 + c % 2][:, m * T:(m + 1) * T], c % 2, k_, slice(m * P, (m + 1) * P),
                                     mhi[:, k_], mlo[:, k_], k_ == 0, k_ == KD - 1)
                last.then_inc(sg["multiplied"], 1)
            ffn(1, N_FFN2, N_DOWN2, 2)
            for g in range(2):
                for i in range(4):
                    c = 4 * g + i
                    pe.wait_ge(sg["gained"], 3 * KD + c // 2 * 2 + 2)
                    for j in range(2):
                        last = nc.tensor.transpose(bank[FINAL[g][j]][:, i * P:(i + 1) * P],
                                                   h_f[:, c, j * P:(j + 1) * P], ident)
                last.then_inc(sg["final_T"], 1)
            mean_square(3, False)


_INS = ("x", "rel_bias", "norm_ffn1", "ffn1_gate", "ffn1_up", "ffn1_down", "norm_mix", "w_in", "mix_rkv",
        "mix_wag", "w_lora_a", "w_lora_b", "w0", "a_lora_a", "a_lora_b", "a0", "g_lora_a", "g_lora_b", "k_k",
        "k_a", "r_k", "ln_x_w", "ln_x_b", "proj_a", "proj_b", "w_out", "norm_ffn2", "ffn2_gate", "ffn2_up",
        "ffn2_down", "norm_final")


def kernel(**inputs):
    import concourse.bacc as bacc
    from concourse.bass_utils import run_bass_kernel_spmd

    nc = bacc.Bacc("TRN2", target_bir_lowering=False, num_devices=1)
    arrays, args = {}, {}
    for name in _INS:
        a = np.ascontiguousarray(inputs[name])
        arrays[f"in_{name}"] = a
        args[name] = nc.dram_tensor(f"in_{name}", a.shape, mybir.dt.from_np(a.dtype), kind="ExternalInput").ap()
    arrays["in_consts"] = shape_constants()
    consts = nc.dram_tensor("in_consts", (P, C_ALL), F32, kind="ExternalInput").ap()
    out = nc.dram_tensor("out_x", (1, T, D), F32, kind="ExternalOutput").ap()
    trunk(nc, args, consts, out)
    r = run_bass_kernel_spmd(nc, [arrays], core_ids=[0])
    return r.results[0]["out_x"]
```
